# Optimizing a Trainium2 kernel written in Bass

```python
import jax
import jax.numpy as jnp
from jax import lax
import numpy as np
import math
import jax, jax.numpy as jnp

D_MODEL = 2048
BATCH = 1
SEQ = 256
DEPTH = 1

GRID_W = 64
CTX_LEN = 256
EPS = 1e-6
CONV_DIM = D_MODEL // 2
CONV_WIDTH = 31
SGU_DIM = D_MODEL // 2
SGU_CHUNK = 128
SGU_GROUPS = SGU_DIM // 128
NA_HEAD_DIM = 64
NA_HEADS = (D_MODEL // 2) // NA_HEAD_DIM
NA_DIM = NA_HEADS * NA_HEAD_DIM
NA_KH = 8
NA_KW = 16
N_BRANCH = 3
D_FF = 4 * D_MODEL
Q_OFF = 2 * CONV_DIM + 2 * SGU_DIM
K_OFF = Q_OFF + NA_DIM
V_OFF = K_OFF + NA_DIM
G_OFF = V_OFF + NA_DIM
IN_DIM = G_OFF + N_BRANCH * D_MODEL
NEG_INF = -1e30


def rms_norm(x, g):
    xf = x.astype(jnp.float32)
    y = xf * lax.rsqrt(jnp.mean(xf * xf, axis=-1, keepdims=True) + EPS)
    return (y * g.astype(jnp.float32)).astype(x.dtype)

def layer_norm(x, g, b):
    xf = x.astype(jnp.float32)
    xc = xf - jnp.mean(xf, axis=-1, keepdims=True)
    var = jnp.mean(xc * xc, axis=-1, keepdims=True)
    return (xc * lax.rsqrt(var + EPS) * g.astype(jnp.float32) + b.astype(jnp.float32)).astype(x.dtype)

def modulate(h, shift, scale):
    return h * (1 + scale[:, None, :]) + shift[:, None, :]

def split_heads(t):
    return t.reshape(t.shape[0], t.shape[1], NA_HEADS, NA_HEAD_DIM)

def conv_branch(a, conv_w, conv_b, ln_g, ln_b, w_out):
    a1, a2 = jnp.split(a, 2, axis=-1)
    u = a1 * jax.nn.sigmoid(a2)
    pad = CONV_WIDTH // 2
    u = lax.conv_general_dilated(u, conv_w[:, None, :], window_strides=(1,), padding=[(pad, pad)],
                                 dimension_numbers=('NWC', 'WIO', 'NWC'),
                                 feature_group_count=CONV_DIM) + conv_b
    u = jax.nn.silu(layer_norm(u, ln_g, ln_b))
    return u @ w_out

def sgu_branch(uv, ln_g, ln_b, w_s, b_s, w_out):
    u, v = jnp.split(jax.nn.gelu(uv), 2, axis=-1)
    v = layer_norm(v, ln_g, ln_b)
    bsz, n, _ = v.shape
    v = v.reshape(bsz, n // SGU_CHUNK, SGU_CHUNK, SGU_GROUPS, SGU_DIM // SGU_GROUPS)
    v = jnp.einsum('gpq,bnqgc->bnpgc', w_s, v) + b_s.T[None, None, :, :, None]
    return (u * v.reshape(bsz, n, SGU_DIM)) @ w_out

def neighbourhood_attention(q, k, v, kc, vc, rpb):
    bsz, s, h, dh = q.shape
    rows = s // GRID_W
    kh = min(NA_KH, rows)
    ncb = GRID_W // NA_KW
    kbw = 2 * NA_KW
    r = np.arange(rows)
    row_idx = np.clip(r - kh // 2, 0, rows - kh)[:, None] + np.arange(kh)[None]
    dr = row_idx - r[:, None]
    j = np.arange(ncb)
    col_idx = np.clip(j * NA_KW - NA_KW // 2, 0, GRID_W - kbw)[:, None] + np.arange(kbw)[None]
    qc = j[:, None] * NA_KW + np.arange(NA_KW)[None]
    win_start = np.clip(qc - NA_KW // 2, 0, GRID_W - NA_KW)
    off = col_idx[:, None, :] - win_start[:, :, None]
    col_valid = (off >= 0) & (off < NA_KW)
    dc = np.clip(col_idx[:, None, :] - qc[:, :, None] + NA_KW - 1, 0, 2 * NA_KW - 2)
    bias = rpb[:, (dr + NA_KH - 1)[:, None, None, :, None], dc[None, :, :, None, :]]
    bias = jnp.where(col_valid[None, None, :, :, None, :], bias.astype(jnp.float32), NEG_INF)

    qg = q.reshape(bsz, rows, ncb, NA_KW, h, dh) * NA_HEAD_DIM ** -0.5
    kg = k.reshape(bsz, rows, GRID_W, h, dh)
    vg = v.reshape(bsz, rows, GRID_W, h, dh)
    ri = row_idx[:, None, :, None]
    ci = col_idx[None, :, None, :]
    k_blk = kg[:, ri, ci]
    v_blk = vg[:, ri, ci]
    s_loc = jnp.einsum('brjqhd,brjiwhd->bhrjqiw', qg, k_blk).astype(jnp.float32) + bias[None]
    s_loc = s_loc.reshape(bsz, h, rows, ncb, NA_KW, kh * kbw)
    s_ctx = jnp.einsum('brjqhd,bchd->bhrjqc', qg, kc).astype(jnp.float32)
    p = jax.nn.softmax(jnp.concatenate([s_loc, s_ctx], axis=-1), axis=-1).astype(v.dtype)
    p_loc = p[..., :kh * kbw].reshape(bsz, h, rows, ncb, NA_KW, kh, kbw)
    p_ctx = p[..., kh * kbw:]
    o = (jnp.einsum('bhrjqiw,brjiwhd->brjqhd', p_loc, v_blk)
         + jnp.einsum('bhrjqc,bchd->brjqhd', p_ctx, vc))
    return o.reshape(bsz, s, NA_DIM)

def context_attention(q, k, v):
    s = jnp.einsum('bqhd,bkhd->bhqk', q * NA_HEAD_DIM ** -0.5, k).astype(jnp.float32)
    p = jax.nn.softmax(s, axis=-1).astype(v.dtype)
    o = jnp.einsum('bhqk,bkhd->bqhd', p, v)
    return o.reshape(o.shape[0], o.shape[1], NA_DIM)

def mixer_output(z, y_na, conv_w, conv_b, conv_ln_g, conv_ln_b, w_conv_out, sgu_ln_g, sgu_ln_b,
                 sgu_w, sgu_b, w_sgu_out, w_na_out, w_o, b_o):
    y_conv = conv_branch(z[..., :2 * CONV_DIM], conv_w, conv_b, conv_ln_g, conv_ln_b, w_conv_out)
    y_sgu = sgu_branch(z[..., 2 * CONV_DIM:Q_OFF], sgu_ln_g, sgu_ln_b, sgu_w, sgu_b, w_sgu_out)
    y_att = y_na @ w_na_out
    g_conv, g_sgu, g_att = jnp.split(jax.nn.sigmoid(z[..., G_OFF:]), N_BRANCH, axis=-1)
    return (g_conv * y_conv + g_sgu * y_sgu + g_att * y_att) @ w_o + b_o

def sq_relu_ffn(h, w1, b1, w2, b2):
    return jnp.square(jax.nn.relu(h @ w1 + b1)) @ w2 + b2

def first_inputs(seed: int = 0) -> dict:
    key = jax.random.key(seed)
    ks = iter(jax.random.split(key, 40))
    f32 = jnp.float32

    def nrm(shape, scale):
        return jax.random.normal(next(ks), shape, f32) * scale

    L = DEPTH
    return {
        'x': nrm((BATCH, SEQ, D_MODEL), 1.0),
        'c': nrm((BATCH, D_MODEL), 1.0),
        'ctx': nrm((BATCH, CTX_LEN, D_MODEL), 1.0),
        'c_ctx': nrm((D_MODEL,), 1.0),
        'w_mod': nrm((L, D_MODEL, 6 * D_MODEL), 0.5 * D_MODEL ** -0.5),
        'b_mod': nrm((L, 6 * D_MODEL), 0.01),
        'norm1_g': 1.0 + nrm((L, D_MODEL), 0.05),
        'norm2_g': 1.0 + nrm((L, D_MODEL), 0.05),
        'w_in': nrm((L, D_MODEL, IN_DIM), D_MODEL ** -0.5),
        'b_in': nrm((L, IN_DIM), 0.01),
        'conv_w': nrm((L, CONV_WIDTH, CONV_DIM), CONV_WIDTH ** -0.5),
        'conv_b': nrm((L, CONV_DIM), 0.01),
        'conv_ln_g': 1.0 + nrm((L, CONV_DIM), 0.05),
        'conv_ln_b': nrm((L, CONV_DIM), 0.01),
        'w_conv_out': nrm((L, CONV_DIM, D_MODEL), CONV_DIM ** -0.5),
        'sgu_ln_g': 1.0 + nrm((L, SGU_DIM), 0.05),
        'sgu_ln_b': nrm((L, SGU_DIM), 0.01),
        'sgu_w': nrm((L, SGU_GROUPS, SGU_CHUNK, SGU_CHUNK), SGU_CHUNK ** -0.5),
        'sgu_b': 1.0 + nrm((L, SGU_GROUPS, SGU_CHUNK), 0.1),
        'w_sgu_out': nrm((L, SGU_DIM, D_MODEL), SGU_DIM ** -0.5),
        'na_rpb': nrm((L, NA_HEADS, 2 * NA_KH - 1, 2 * NA_KW - 1), 0.5),
        'w_na_out': nrm((L, NA_DIM, D_MODEL), NA_DIM ** -0.5),
        'w_o': nrm((L, D_MODEL, D_MODEL), D_MODEL ** -0.5),
        'b_o': nrm((L, D_MODEL), 0.01),
        'w_ff1': nrm((L, D_MODEL, D_FF), D_MODEL ** -0.5),
        'b_ff1': nrm((L, D_FF), 0.01),
        'w_ff2': nrm((L, D_FF, D_MODEL), D_FF ** -0.5),
        'b_ff2': nrm((L, D_MODEL), 0.01),
        'final_g': 1.0 + nrm((D_MODEL,), 0.05),
    }

def first_block(x, c, ctx, c_ctx, w_mod, b_mod, norm1_g, norm2_g, w_in, b_in, conv_w, conv_b,
              conv_ln_g, conv_ln_b, w_conv_out, sgu_ln_g, sgu_ln_b, sgu_w, sgu_b, w_sgu_out,
              na_rpb, w_na_out, w_o, b_o, w_ff1, b_ff1, w_ff2, b_ff2, final_g):
    silu_c = jax.nn.silu(c)
    silu_cc = jax.nn.silu(c_ctx)[None]
    xl, xc = x, ctx
    for l in range(DEPTH):
        last = l == DEPTH - 1
        mod_l = jnp.split(silu_c @ w_mod[l] + b_mod[l], 6, axis=-1)
        mod_c = jnp.split(silu_cc @ w_mod[l] + b_mod[l], 6, axis=-1)
        branch_params = (conv_w[l], conv_b[l], conv_ln_g[l], conv_ln_b[l], w_conv_out[l],
                         sgu_ln_g[l], sgu_ln_b[l], sgu_w[l], sgu_b[l], w_sgu_out[l],
                         w_na_out[l], w_o[l], b_o[l])
        hl = modulate(rms_norm(xl, norm1_g[l]), mod_l[0], mod_l[1])
        hc = modulate(rms_norm(xc, norm1_g[l]), mod_c[0], mod_c[1])
        zl = hl @ w_in[l] + b_in[l]
        if last:
            zkv = hc @ w_in[l, :, K_OFF:G_OFF] + b_in[l, K_OFF:G_OFF]
            kc, vc = split_heads(zkv[..., :NA_DIM]), split_heads(zkv[..., NA_DIM:])
        else:
            zc = hc @ w_in[l] + b_in[l]
            kc, vc = split_heads(zc[..., K_OFF:V_OFF]), split_heads(zc[..., V_OFF:G_OFF])
        y_na_l = neighbourhood_attention(split_heads(zl[..., Q_OFF:K_OFF]), split_heads(zl[..., K_OFF:V_OFF]),
                                         split_heads(zl[..., V_OFF:G_OFF]), kc, vc, na_rpb[l])
        xl = xl + mod_l[2][:, None, :] * mixer_output(zl, y_na_l, *branch_params)
        hl2 = modulate(rms_norm(xl, norm2_g[l]), mod_l[3], mod_l[4])
        xl = xl + mod_l[5][:, None, :] * sq_relu_ffn(hl2, w_ff1[l], b_ff1[l], w_ff2[l], b_ff2[l])
        if not last:
            y_na_c = context_attention(split_heads(zc[..., Q_OFF:K_OFF]), kc, vc)
            xc = xc + mod_c[2][:, None, :] * mixer_output(zc, y_na_c, *branch_params)
            hc2 = modulate(rms_norm(xc, norm2_g[l]), mod_c[3], mod_c[4])
            xc = xc + mod_c[5][:, None, :] * sq_relu_ffn(hc2, w_ff1[l], b_ff1[l], w_ff2[l], b_ff2[l])
    return rms_norm(xl, final_g)


DEPTH_2 = 2

CHUNK = 64
N_META = 16
Q_BLOCK = 128
N_MIXERS = 2
RMS_EPS = 1e-6

DA_HEADS = 8
DA_HEAD_DIM = D_MODEL // (2 * DA_HEADS)
DA_V_DIM = 2 * DA_HEAD_DIM
ROPE_THETA = 500000.0
ROPE_DIM = DA_HEAD_DIM // 4

POOL_WINDOWS = (2, 4, 8, 16)
POOL_GROUPS = len(POOL_WINDOWS)
POOL_GROUP_DIM = D_MODEL // POOL_GROUPS

N_ATTN_LAYERS = (DEPTH_2 + 1) // 2
N_POOL_LAYERS = DEPTH_2 // 2


def rms_norm_2(x, g):
    xf = x.astype(jnp.float32)
    y = xf * lax.rsqrt(jnp.mean(xf * xf, axis=-1, keepdims=True) + RMS_EPS)
    return (y * g.astype(jnp.float32)).astype(x.dtype)

def chunk_ids(length):
    p = jnp.arange(length)
    return jnp.where(p < N_META, 0, (p - N_META) // CHUNK + 1)

def rope_tables(length):
    pos = jnp.arange(length, dtype=jnp.float32)
    inv = ROPE_THETA ** (-jnp.arange(0, ROPE_DIM, 2, dtype=jnp.float32) / ROPE_DIM)
    ang = pos[:, None] * inv[None, :]
    return jnp.cos(ang), jnp.sin(ang)

def apply_partial_rope(t, cos, sin):
    half = ROPE_DIM // 2
    c = cos.astype(t.dtype)
    s = sin.astype(t.dtype)
    r1 = t[..., :half]
    r2 = t[..., half:ROPE_DIM]
    return jnp.concatenate([r1 * c - r2 * s, r2 * c + r1 * s, t[..., ROPE_DIM:]], axis=-1)

def diff_attend(q1, q2, k1, k2, v, qc, kc, lam):
    scale = DA_HEAD_DIM ** -0.5
    mask = kc[None, :] <= qc[:, None]
    neg = jnp.finfo(jnp.float32).min
    s1 = jnp.einsum('bhqd,bhkd->bhqk', q1, k1).astype(jnp.float32) * scale
    s2 = jnp.einsum('bhqd,bhkd->bhqk', q2, k2).astype(jnp.float32) * scale
    p1 = jax.nn.softmax(jnp.where(mask, s1, neg), axis=-1)
    p2 = jax.nn.softmax(jnp.where(mask, s2, neg), axis=-1)
    a = p1 - lam * p2
    return jnp.einsum('bhqk,bhkd->bhqd', a.astype(v.dtype), v)

def diff_attention_mixer(h, w_in, w_out, lq1, lk1, lq2, lk2, subln_g, layer_idx, cos, sin):
    B, L, D = h.shape
    proj = h @ w_in
    q, k, v, g = jnp.split(proj, 4, axis=-1)
    q = q.reshape(B, L, DA_HEADS, 2, DA_HEAD_DIM).transpose(0, 2, 3, 1, 4)
    k = k.reshape(B, L, DA_HEADS, 2, DA_HEAD_DIM).transpose(0, 2, 3, 1, 4)
    v = v.reshape(B, L, DA_HEADS, DA_V_DIM).transpose(0, 2, 1, 3)
    q1 = apply_partial_rope(q[:, :, 0], cos, sin)
    q2 = apply_partial_rope(q[:, :, 1], cos, sin)
    k1 = apply_partial_rope(k[:, :, 0], cos, sin)
    k2 = apply_partial_rope(k[:, :, 1], cos, sin)

    lam_init = 0.8 - 0.6 * math.exp(-0.3 * layer_idx)
    lam = (jnp.exp(jnp.sum(lq1.astype(jnp.float32) * lk1.astype(jnp.float32)))
           - jnp.exp(jnp.sum(lq2.astype(jnp.float32) * lk2.astype(jnp.float32)))
           + lam_init)

    cid = chunk_ids(L)
    outs = [diff_attend(q1[:, :, :N_META], q2[:, :, :N_META], k1[:, :, :N_META],
                        k2[:, :, :N_META], v[:, :, :N_META], cid[:N_META], cid[:N_META], lam)]
    n_blocks = (L - N_META) // Q_BLOCK
    for b in range(n_blocks):
        q0 = N_META + b * Q_BLOCK
        q1e = q0 + Q_BLOCK
        outs.append(diff_attend(q1[:, :, q0:q1e], q2[:, :, q0:q1e], k1[:, :, :q1e],
                                k2[:, :, :q1e], v[:, :, :q1e], cid[q0:q1e], cid[:q1e], lam))
    o = jnp.concatenate(outs, axis=2)
    o = rms_norm_2(o, subln_g) * (1.0 - lam_init)
    o = o.transpose(0, 2, 1, 3).reshape(B, L, D)
    return (o * jax.nn.silu(g)) @ w_out

def pool_mixer(h, w_in, w_group, scale, w_out):
    B, L, D = h.shape
    proj = h @ w_in
    u, g = jnp.split(proj, 2, axis=-1)
    ug = u.reshape(B, L, POOL_GROUPS, POOL_GROUP_DIM)
    cs = jnp.cumsum(ug.astype(jnp.float32), axis=1)
    csp = jnp.concatenate([jnp.zeros((B, 1, POOL_GROUPS, POOL_GROUP_DIM), jnp.float32), cs], axis=1)
    t = jnp.arange(L)
    pooled = []
    for gi, w in enumerate(POOL_WINDOWS):
        start = jnp.maximum(t + 1 - w, 0)
        cnt = jnp.minimum(t + 1, w).astype(jnp.float32)
        s = csp[:, 1:, gi] - csp[:, start, gi]
        pooled.append(s / cnt[None, :, None])
    pooled = jnp.stack(pooled, axis=2).astype(u.dtype)
    mixed = pooled - ug
    mixed = jnp.einsum('blgc,gcd->blgd', mixed, w_group).reshape(B, L, D) * scale
    return (mixed * jax.nn.silu(g)) @ w_out

def second_inputs(seed: int = 0) -> dict:
    key = jax.random.key(seed)
    ks = jax.random.split(key, 16)
    D = D_MODEL
    f = jnp.float32
    nrm = jax.random.normal
    return {
        "x": nrm(ks[0], (BATCH, SEQ, D), f),
        "meta_tokens": nrm(ks[1], (N_META, D), f),
        "pre_norm_g": 1.0 + 0.05 * nrm(ks[2], (DEPTH_2, D), f),
        "post_norm_g": 1.0 + 0.05 * nrm(ks[3], (DEPTH_2, D), f),
        "attn_w_in": nrm(ks[4], (N_ATTN_LAYERS, D, 4 * D), f) * D ** -0.5,
        "attn_w_out": nrm(ks[5], (N_ATTN_LAYERS, D, D), f) * D ** -0.5,
        "attn_lambda_q1": 0.1 * nrm(ks[6], (N_ATTN_LAYERS, DA_HEAD_DIM), f),
        "attn_lambda_k1": 0.1 * nrm(ks[7], (N_ATTN_LAYERS, DA_HEAD_DIM), f),
        "attn_lambda_q2": 0.1 * nrm(ks[8], (N_ATTN_LAYERS, DA_HEAD_DIM), f),
        "attn_lambda_k2": 0.1 * nrm(ks[9], (N_ATTN_LAYERS, DA_HEAD_DIM), f),
        "attn_subln_g": 1.0 + 0.05 * nrm(ks[10], (N_ATTN_LAYERS, DA_V_DIM), f),
        "pool_w_in": nrm(ks[11], (N_POOL_LAYERS, D, 2 * D), f) * D ** -0.5,
        "pool_w_group": nrm(ks[12], (N_POOL_LAYERS, POOL_GROUPS, POOL_GROUP_DIM, POOL_GROUP_DIM), f) * POOL_GROUP_DIM ** -0.5,
        "pool_scale": 1.0 + 0.1 * nrm(ks[13], (N_POOL_LAYERS, D), f),
        "pool_w_out": nrm(ks[14], (N_POOL_LAYERS, D, D), f) * D ** -0.5,
    }

def second_block(x, meta_tokens, pre_norm_g, post_norm_g, attn_w_in, attn_w_out,
              attn_lambda_q1, attn_lambda_k1, attn_lambda_q2, attn_lambda_k2, attn_subln_g,
              pool_w_in, pool_w_group, pool_scale, pool_w_out):
    B = x.shape[0]
    meta = jnp.broadcast_to(meta_tokens.astype(x.dtype)[None], (B, N_META, x.shape[-1]))
    h = jnp.concatenate([meta, x], axis=1)
    L = h.shape[1]
    cos, sin = rope_tables(L)
    for i in range(DEPTH_2):
        j = i // N_MIXERS
        hn = rms_norm_2(h, pre_norm_g[i])
        if i % N_MIXERS == 0:
            y = diff_attention_mixer(hn, attn_w_in[j], attn_w_out[j], attn_lambda_q1[j],
                                     attn_lambda_k1[j], attn_lambda_q2[j], attn_lambda_k2[j],
                                     attn_subln_g[j], i, cos, sin)
        else:
            y = pool_mixer(hn, pool_w_in[j], pool_w_group[j], pool_scale[j], pool_w_out[j])
        h = h + rms_norm_2(y, post_norm_g[i])
    return h[:, N_META:]


def setup_inputs(seed=0):
    out = dict(first_inputs(seed))
    for name, value in second_inputs(seed + 1).items():
        if name != "x":
            out[name + "_2"] = value
    return out


def reference(
    x, c, ctx, c_ctx, w_mod, b_mod, norm1_g, norm2_g, w_in, b_in, conv_w, conv_b, conv_ln_g,
    conv_ln_b, w_conv_out, sgu_ln_g, sgu_ln_b, sgu_w, sgu_b, w_sgu_out, na_rpb, w_na_out, w_o,
    b_o, w_ff1, b_ff1, w_ff2, b_ff2, final_g, meta_tokens_2, pre_norm_g_2, post_norm_g_2,
    attn_w_in_2, attn_w_out_2, attn_lambda_q1_2, attn_lambda_k1_2, attn_lambda_q2_2,
    attn_lambda_k2_2, attn_subln_g_2, pool_w_in_2, pool_w_group_2, pool_scale_2, pool_w_out_2,
):
    x = first_block(
        x, c, ctx, c_ctx, w_mod, b_mod, norm1_g, norm2_g, w_in, b_in, conv_w, conv_b, conv_ln_g,
        conv_ln_b, w_conv_out, sgu_ln_g, sgu_ln_b, sgu_w, sgu_b, w_sgu_out, na_rpb, w_na_out,
        w_o, b_o, w_ff1, b_ff1, w_ff2, b_ff2, final_g,
    )
    return second_block(
        x, meta_tokens_2, pre_norm_g_2, post_norm_g_2, attn_w_in_2, attn_w_out_2,
        attn_lambda_q1_2, attn_lambda_k1_2, attn_lambda_q2_2, attn_lambda_k2_2, attn_subln_g_2,
        pool_w_in_2, pool_w_group_2, pool_scale_2, pool_w_out_2,
    )


_drawn_inputs = setup_inputs


def setup_inputs(seed=0):
    import zlib

    import numpy as np

    out = dict(_drawn_inputs(seed))
    spreads = {}
    factors = {'norm1_g': 2.981,
     'b_in': 7.701,
     'conv_b': 27.21,
     'conv_ln_g': 14.56,
     'conv_ln_b': 64.0,
     'sgu_ln_g': 6.454,
     'sgu_ln_b': 25.197,
     'sgu_b': 3.323,
     'na_rpb': 6.906,
     'b_o': 27.452,
     'b_ff1': 19.225,
     'b_ff2': 26.368,
     'attn_lambda_q1_2': 8.0,
     'norm2_g': 3.82}
    for name, (base, spread) in spreads.items():
        noise = np.random.default_rng([zlib.crc32(name.encode()), seed]).standard_normal(out[name].shape)
        drawn = base * np.exp(spread * noise) if base else spread * noise
        out[name] = jnp.asarray(drawn.astype(out[name].dtype))
    for name, factor in factors.items():
        out[name] = (out[name] * factor).astype(out[name].dtype)
    return out
```

```python
from collections import deque
from contextlib import ExitStack

import numpy as np

import concourse.bass as bass
from concourse import mybir

F32 = mybir.dt.float32
F32R = mybir.dt.float32r
ALU = mybir.AluOpType
ACT = mybir.ActivationFunctionType
AX = mybir.AxisListType

D = 2048
T = 256
NM = 16
L = T + NM
KU = 8
NRAW = 4
NSPLIT = 5
AHEAD = 3
EPS = 1e-6
SCALE2 = 128.0 ** -0.5
NEG = -1e30

VECS = [("c", 16), ("cc", 16), ("b_mod", 96), ("n1g", 16), ("n2g", 16), ("b_in", 104), ("conv_b", 8),
        ("cln_g", 8), ("cln_b", 8), ("conv_w", 248), ("sln_g", 8), ("sln_b", 8), ("b_o", 16),
        ("b_ff1", 64), ("b_ff2", 16), ("fin_g", 16), ("pre_g", 32), ("post_g", 32), ("sub_g", 2),
        ("p_scale", 16), ("lam", 4)]
VOFF = {}
_at = 0
for _n, _w in VECS:
    VOFF[_n] = _at
    _at += _w
NVEC = _at
C_ID, C_MASK, C_COS, C_SIN, C_ONE, C_EPS = 0, 128, 192, 192 + L, 192 + 2 * L, 193 + 2 * L
NCONST = 194 + 2 * L


class Engine:

    def __init__(self, sem):
        self.sem, self.count, self.items, self.seen = sem, 0, [], {}

    def put(self, fn, *after, mark=True, inc=None):
        waits = []
        for t in flat(after):
            sem, v = t
            if self.seen.get(id(sem), 0) < v:
                self.seen[id(sem)] = v
                waits.append(t)
        if inc is None and mark:
            self.count += 1
            inc = (self.sem, 1)
        self.items.append((waits, fn, inc))
        return (self.sem, self.count) if mark else None

    def run(self, eng):
        for waits, fn, inc in self.items:
            for sem, v in waits:
                eng.wait_ge(sem, v)
            ins = fn(eng)
            if inc is not None:
                ins.then_inc(*inc)


def flat(x):
    for t in x:
        if t is None:
            continue
        if isinstance(t, list):
            yield from flat(t)
        else:
            yield t


class Buf:

    def __init__(self, ap):
        self.ap, self.after, self.held = ap, [], False

    @property
    def free(self):
        return self.after

    @free.setter
    def free(self, after):
        self.after, self.held = after, False


class Ring:
    def __init__(self, aps):
        self.bufs, self.n = [Buf(a) for a in aps], 0

    def get(self):
        for _ in self.bufs:
            b = self.bufs[self.n % len(self.bufs)]
            self.n += 1
            if not b.held:
                b.held = True
                return b
        raise ValueError("all of a ring's buffers are held")


def unit_plan():
    plan = []

    def full(name, m, kh=2):
        for h in range(kh):
            plan.append((name, m, h))

    mod = deque(("mod", nb, q) for nb in range(8, 24) for q in range(8))
    for nb in range(8):
        for q in range(8):
            plan.append(("mod0", nb, q))
    for m in list(range(40, 56)) + list(range(32, 40)) + list(range(24, 32)):
        full("w_in", m)
    for m in range(8):
        full("w_in", m)
        full("w_in", 8 + m)
    for m in range(16, 24):
        full("w_in", m)
    for g0, name in ((72, "w_sgu"), (88, "w_na"), (56, "w_conv")):
        for m in range(16):
            full("w_in", g0 + m)
            full(name, m, 1)
    for m in range(16):
        full("w_o", m)
    for c in range(4):
        for m in range(16):
            full("w_ff1", 16 * c + m)
        for m in range(16):
            plan.append(("w_ff2", m, 2 * c))
            plan.append(("w_ff2", m, 2 * c + 1))
    out = []
    for i, u in enumerate(plan):
        out.append(u)
        for _ in range(2 if 64 <= i < 96 else 1 if i >= 176 and i % 3 == 0 else 0):
            if mod:
                out.append(mod.popleft())
    assert not mod and out.index(("mod", 19, 7)) < out.index(("w_o", 14, 0))
    plan = out
    for h in range(8):
        for m in (16 + 2 * h, 17 + 2 * h, 2 * h, 2 * h + 1, 32 + 2 * h, 33 + 2 * h, 48 + 2 * h, 49 + 2 * h):
            full("w_ain", m)
    for m in range(16):
        full("w_aout", m)
    for m in range(32):
        full("w_pin", m)
    for g in range(4):
        plan += [("w_grp", g, 0), ("w_grp", g, 1)]
    for m in range(16):
        full("w_pout", m)
    return plan


def build(nc, ar, out_d):
    ctx = ExitStack()
    with ctx:
        def sem(name):
            return ctx.enter_context(nc.semaphore(name))

        def sb(name, shape, dt=F32, stack=ctx, side="left"):
            return stack.enter_context(nc.sbuf_tensor(name, shape, dt, side=side))

        PE, V, S, G, SP = (Engine(sem(n)) for n in ("s_pe", "s_dve", "s_act", "s_pool", "s_sp"))

        vec = sb("vec", [128, NVEC])
        cst = sb("cst", [128, NCONST])
        modv = sb("modv", [128, 128])
        vt = sb("vt", [128, 256])
        H = sb("H", [128, 16, L])
        AH, AL = sb("AH", [128, 16, L], F32R), sb("AL", [128, 16, L], F32R)
        raws = [sb(f"raw{i}", [128, KU * 128]) for i in range(NRAW)]
        his = [sb(f"hi{i}", [128, KU, 128], F32R) for i in range(NSPLIT)]
        los = [sb(f"lo{i}", [128, KU, 128], F32R) for i in range(NSPLIT)]
        tmp = Ring([sb(f"tmp{i}", [128, L]) for i in range(7)])
        sqr = Ring([sb(f"sqr{i}", [128, L]) for i in range(2)])
        ssum = Buf(sb("ssum", [128, L]))
        rows = Ring([sb(f"row{i}", [128, L]) for i in range(2)])
        st4 = Ring([sb(f"st{i}", [128, 4]) for i in range(6)])
        onesD = {n: sb(f"ones{n}", [128, 128]) for n in (2048, 1024, 256)}

        banks = [Buf(ctx.enter_context(nc.psum_tensor(f"ps{i}", [128, 512], F32))) for i in range(8)]
        acc = Ring([])
        acc.bufs = banks[0:4]
        S0, S1, TB, XB = banks[4:8]

        ident = cst[:, C_ID:C_ID + 128]
        one = cst[:, C_ONE:C_ONE + 1]
        eps = cst[:, C_EPS:C_EPS + 1]

        def col(name, i, rows_=slice(0, 128)):
            o = VOFF[name] + i
            return vec[rows_, o:o + 1]

        def cols(name, n, at=0):
            o = VOFF[name] + at
            return vec[:, o:o + n]

        def load(dst, src, *after):
            s = sem(f"s_ld{len(loads)}")
            loads.append(s)
            SP.put(lambda e: e.dma_start(dst, src), *after, mark=False, inc=(s, 16))
            return (s, 16)

        loads = []
        t_vec = load(vec[:, :], ar["vec"])
        t_cst = load(cst[:, :], ar["cst"])

        plan = unit_plan()
        raw_sem = [sem(f"s_raw{i}") for i in range(NRAW)]
        raw_free = [[] for _ in range(NRAW)]
        split_free = [[] for _ in range(NSPLIT)]
        st = {"dma": 0, "split": 0, "use": 0, "nsplit": 0}
        split_of = {}

        def issue(n=1):
            for _ in range(n):
                i = st["dma"]
                if i >= len(plan):
                    return
                st["dma"] += 1
                name, m, h = plan[i]
                src = ar["w_mod"][m, h] if name in ("mod", "mod0") else ar[name][m, h]
                dst = raws[i % NRAW][:, :]
                SP.put(lambda e, d=dst, s=src: e.dma_start(d, s), raw_free[i % NRAW], mark=False,
                       inc=(raw_sem[i % NRAW], 16))

        def landed(i):
            return (raw_sem[i % NRAW], 16 * (i // NRAW + 1))

        issue(NRAW)
        t_x = load(H[:, :, NM:L], ar["x"])
        t_meta = load(H[:, :, 0:NM], ar["meta"])

        def split_unit(i):
            s = st["nsplit"] % NSPLIT
            st["nsplit"] += 1
            r = raws[i % NRAW]
            src = r[:, :].rearrange("p (k m) -> p k m", k=KU)
            hi, lo = his[s], los[s]
            t_hi = S.put(lambda e: e.activation(hi[:, :, :], src, ACT.Copy), landed(i), split_free[s])
            t_lo = V.put(lambda e: e.tensor_tensor(lo[:, :, :], src, hi[:, :, :].bitcast(F32), ALU.subtract),
                         landed(i), t_hi, split_free[s])
            raw_free[i % NRAW] = [t_lo, t_hi]
            issue()
            split_of[i] = (s, t_hi, t_lo)

        gemv = {}

        def advance(ahead):
            while st["split"] < len(plan) and st["split"] <= st["use"] + ahead:
                i = st["split"]
                name = plan[i][0]
                if name == "mod0":
                    return
                st["split"] += 1
                if name == "mod":
                    mod_unit(i)
                else:
                    split_unit(i)

        def use(key):
            while plan[st["use"]][0] == "mod":
                st["use"] += 1
            i = st["use"]
            assert plan[i] == key, (plan[i], key)
            n_mod = sum(plan[j][0] == "mod" for j in range(i, min(i + AHEAD + 3, len(plan))))
            advance(AHEAD + min(n_mod, 2))
            st["use"] += 1
            s, t_hi, t_lo = split_of.pop(i)
            return s, t_hi, t_lo

        active = []

        def spawn(gen):
            active.append(gen)
            return gen

        def step():
            for g in list(active):
                if next(g, StopIteration) is StopIteration:
                    active.remove(g)

        def finish(*gens):
            for g in gens:
                while g in active:
                    step()

        def gemm(name, ms, halves, rhs, ready, n, bank=None, group=None):
            b = acc.get() if bank is None else bank
            first, tok = True, None
            for hi_, h in enumerate(halves):
                s, t_hi, t_lo = use((name, ms, h))
                for k in range(KU):
                    kt = hi_ * KU + k
                    parts = rhs(kt)
                    for j, (xh, xl, o) in enumerate(parts):
                        for q, (w, x, t) in enumerate(((his[s], xh, t_hi), (his[s], xl, None), (los[s], xh, t_lo))):
                            last = hi_ == len(halves) - 1 and k == KU - 1 and q == 2 and j == len(parts) - 1
                            ul = k == KU - 1 and q == 2 and j == len(parts) - 1
                            f, first = first, False
                            tok = PE.put(lambda e, o=o, w=w, x=x, k=k, f=f, z=(hi_ == len(halves) - 1 and k == KU - 1 and q == 2):
                                         e.matmul(b.ap[:, o], w[:, k, :], x, start=f, stop=z,
                                                  skip_group_check=len(parts) > 1),
                                         [t] if j == 0 else [], ready(kt) if q == 0 and j == 0 else [],
                                         b.free if f else [], mark=ul) or tok
                split_free[s] = [tok]
                step()
            return b, tok

        def split(src, hi, lo, after, free=(), scale=1.0, eng=None):
            if eng is V:
                th = V.put(lambda e: e.tensor_copy(hi, src), after, *free)
            else:
                th = S.put(lambda e: e.activation(hi, src, ACT.Copy, scale=scale), after, *free)
            if scale == 1.0:
                tl = V.put(lambda e: e.tensor_tensor(lo, src, hi.bitcast(F32), ALU.subtract), after, th, *free)
            else:
                tl = V.put(lambda e: e.scalar_tensor_tensor(out=lo, in0=src, scalar=scale, in1=hi.bitcast(F32),
                                                            op0=ALU.mult, op1=ALU.subtract), after, th, *free)
            return [th, tl]

        def split_later(src, hi, lo, after, free=(), scale=1.0):
            th = S.put(lambda e: e.activation(hi, src, ACT.Copy, scale=scale), after, *free)
            yield
            if scale == 1.0:
                tl = V.put(lambda e: e.tensor_tensor(lo, src, hi.bitcast(F32), ALU.subtract), after, th, *free)
            else:
                tl = V.put(lambda e: e.scalar_tensor_tensor(out=lo, in0=src, scalar=scale, in1=hi.bitcast(F32),
                                                            op0=ALU.mult, op1=ALU.subtract), after, th, *free)
            return [th, tl]

        t_ones = [V.put(lambda e, n=n, o=o: e.memset(o[:, :], 1.0 / n)) for n, o in onesD.items()]
        SC, HB, BQ, G1, G1C, G2M, LAMC, SG, PB = 0, 32, 136, 144, 160, 176, 192, 196, 200
        scv = vt[:, SC:SC + 32].rearrange("p (k t) -> p t k", t=2)
        tm = tmp.get()
        a = S.put(lambda e: e.activation(tm.ap[:, 0:32], vec[:, 0:32], ACT.Tanh, scale=0.5), t_vec)
        a = V.put(lambda e: e.tensor_scalar(tm.ap[:, 32:64], tm.ap[:, 0:32], 1.0, 0.5, ALU.add, ALU.mult), a)
        t_sc = V.put(lambda e: e.tensor_tensor(scv, tm.ap[:, 32:64].rearrange("p (t k) -> p t k", t=2),
                                               vec[:, 0:32].rearrange("p (t k) -> p t k", t=2), ALU.mult), a, t_vec)
        tm.free = [t_sc]
        t_hb = V.put(lambda e: e.tensor_scalar(vt[:, HB:HB + 104], cols("b_in", 104), 0.5, None, ALU.mult), t_vec)
        t_bq = V.put(lambda e: e.tensor_scalar(vt[:, BQ:BQ + 8], cols("b_in", 8, 32), 0.125, None, ALU.mult), t_vec)
        t_cw = V.put(lambda e: e.tensor_scalar(cols("conv_w", 248), cols("conv_w", 248), 0.5, None, ALU.mult), t_vec)
        a = V.put(lambda e: e.tensor_tensor(vt[:, LAMC:LAMC + 2], cols("lam", 2), cols("lam", 2, 2), ALU.mult), t_vec)
        onesf = sb("onesf", [128, 128])
        t_of = V.put(lambda e: e.memset(onesf[:, :], 1.0))
        a = PE.put(lambda e: e.matmul(XB.ap[:, 0:2], onesf[:, :], vt[:, LAMC:LAMC + 2], start=True, stop=True), a, t_of)
        a = S.put(lambda e: e.activation(vt[:, LAMC + 2:LAMC + 4], XB.ap[:, 0:2], ACT.Exp), a)
        XB.free = [a]
        a = V.put(lambda e: e.tensor_tensor(vt[:, LAMC:LAMC + 1], vt[:, LAMC + 2:LAMC + 3], vt[:, LAMC + 3:LAMC + 4],
                                            ALU.subtract), a)
        t_lam = V.put(lambda e: e.tensor_scalar(vt[:, LAMC:LAMC + 1], vt[:, LAMC:LAMC + 1], 0.2, None, ALU.add), a)
        t_sg = V.put(lambda e: e.tensor_scalar(vt[:, SG:SG + 2], cols("sub_g", 2), 0.8, 0.5, ALU.mult, ALU.mult), t_vec)
        t_ps = V.put(lambda e: e.tensor_scalar(vt[:, PB:PB + 16], cols("p_scale", 16), 0.5, None, ALU.mult), t_vec)

        def add_up(first, src, after, n):
            if first:
                t = G.put(lambda e: e.tensor_copy(ssum.ap[:, 0:n], src), after, ssum.free)
            else:
                t = G.put(lambda e: e.tensor_tensor(ssum.ap[:, 0:n], ssum.ap[:, 0:n], src, ALU.add), after,
                          (G.sem, G.count))
            return t

        def square_up(first, src, after, n):
            q = sqr.get()
            a = S.put(lambda e: e.activation(q.ap[:, 0:n], src, ACT.Square), after, q.free)
            t = add_up(first, q.ap[:, 0:n], a, n)
            q.free = [t]
            return a, t

        def inv_root(d, n, after):
            r = rows.get()
            p = PE.put(lambda e: e.matmul(XB.ap[:, 0:n], onesD[d][:, :], ssum.ap[:, 0:n], start=True, stop=True),
                       after, t_ones, XB.free)
            ssum.free = [p]
            a = S.put(lambda e: e.activation(r.ap[:, 0:n], XB.ap[:, 0:n], ACT.Sqrt, bias=eps), p, r.free, t_cst)
            XB.free = [a]
            t = V.put(lambda e: e.reciprocal(r.ap[:, 0:n], r.ap[:, 0:n]), a)
            return r, t

        macc = Ring([sb(f"macc{i}", [128, 512]) for i in range(2)])

        def mod_unit(i):
            _, nb, q = plan[i]
            if q == 0:
                gemv["buf"] = macc.get()
            m = gemv["buf"]
            r = raws[i % NRAW]
            tok = gemv.get("tok")
            for j in range(2):
                k = 2 * q + j
                w = r[:, 512 * j:512 * j + 512]
                s = vt[:, SC + 2 * k:SC + 2 * k + 1]
                if k == 0:
                    tok = V.put(lambda e, w=w, s=s: e.tensor_scalar(m.ap[:, :], w, s, None, ALU.mult), landed(i), m.free, t_sc)
                else:
                    tok = V.put(lambda e, w=w, s=s: e.scalar_tensor_tensor(
                        out=m.ap[:, :], in0=w, scalar=s, in1=m.ap[:, :], op0=ALU.mult, op1=ALU.add),
                        landed(i), tok)
            gemv["tok"] = tok
            raw_free[i % NRAW] = [tok]
            issue()
            if q == 7:
                spawn(mod_out(nb, m, tok))

        t_modv = {}

        def mod_out(nb, m, tok):
            yield
            for j in range(4):
                p = PE.put(lambda e, j=j: e.matmul(XB.ap[:, j:j + 1], m.ap[:, 128 * j:128 * j + 128], one,
                                                   start=True, stop=True), tok, XB.free, t_cst)
            m.free = [p]
            t = V.put(lambda e: e.tensor_tensor(modv[:, 4 * nb:4 * nb + 4], XB.ap[:, 0:4], cols("b_mod", 4, 4 * nb),
                                                ALU.add), p, t_vec)
            XB.free = [t]
            t_modv[nb] = t
            yield

        early = ExitStack()
        mrow = Ring([sb(f"mrow{i}", [2, 512], F32, early, "right") for i in range(2)])

        def mod_turn(nb, r, t):
            for j in range(4):
                p = PE.put(lambda e, j=j: e.matmul(XB.ap[:, 2 * j:2 * j + 2], r.ap[0:2, 128 * j:128 * j + 128],
                                                   ident[0:2, 0:2], start=True, stop=True), t, XB.free, t_cst)
            r.free = [p]
            pv = XB.ap[:, 0:8].rearrange("p (j t) -> p t j", t=2)
            a = V.put(lambda e: e.tensor_tensor(modv[:, 4 * nb:4 * nb + 4], pv[:, 0, :], cols("b_mod", 4, 4 * nb),
                                                ALU.add), p, t_vec)
            a = V.put(lambda e: e.tensor_tensor(modv[:, 96 + 4 * nb:100 + 4 * nb], pv[:, 1, :],
                                                cols("b_mod", 4, 4 * nb), ALU.add))
            XB.free = [a]
            return a

        phase = ExitStack()
        G16 = sb("G16", [128, 16 * T])
        ctxv = G16[:, :].rearrange("p (k t) -> p k t", k=16)
        CH, CL = (sb(n, [128, 16, T], F32R, early, "right") for n in ("CH", "CL"))
        VTok = sb("VTok", [128, 4, 1024], F32, phase)
        t_ctx = load(ctxv, ar["ctx"])

        def norms():
            rr = []
            for src, t_in, o in ((H[:, :, NM:L], t_x, 0), (ctxv, t_ctx, 0)):
                for k in range(16):
                    _, t = square_up(k == 0, src[:, k, :], t_in, T)
                    if k % 2:
                        yield
                rr.append(inv_root(2048, T, t))
                yield
            norm_rows.extend(rr)

        norm_rows = []
        pending = None
        spawn(norms())
        for nb in range(8):
            b = acc.get()
            for q in range(8):
                i = st["use"]
                assert plan[i] == ("mod0", nb, q)
                st["use"] += 1
                st["split"] = st["use"]
                for j in range(2):
                    k = 2 * q + j
                    p = PE.put(lambda e, b=b, i=i, j=j, k=k: e.matmul(
                        b.ap[0:2, :], vt[:, SC + 2 * k:SC + 2 * k + 2], raws[i % NRAW][:, 512 * j:512 * j + 512],
                        start=(k == 0), stop=(k == 15)), landed(i), t_sc, b.free, mark=(j == 1))
                raw_free[i % NRAW] = [p]
                issue()
                if q % 2:
                    step()
            if pending:
                t_m = mod_turn(*pending)
            r = mrow.get()
            t = S.put(lambda e, r=r, b=b: e.activation(r.ap[:, :], b.ap[0:2, :], ACT.Copy), p, r.free)
            b.free = [t]
            pending = (nb, r, t)
        t_m = mod_turn(*pending)
        finish(*active)
        (rx, t_rx), (rc, t_rc) = norm_rows

        t_g1 = V.put(lambda e: e.scalar_tensor_tensor(out=vt[:, G1:G1 + 16], in0=modv[:, 16:32], scalar=1.0,
                                                      in1=cols("n1g", 16), op0=ALU.add, op1=ALU.mult), t_m)
        t_g1c = V.put(lambda e: e.scalar_tensor_tensor(out=vt[:, G1C:G1C + 16], in0=modv[:, 112:128], scalar=1.0,
                                                       in1=cols("n1g", 16), op0=ALU.add, op1=ALU.mult), t_m)

        def modulated(k, src, row, t_row, n, hi, lo, gain, shift, t_gain, free=()):
            m = tmp.get()
            a = V.put(lambda e: e.tensor_tensor(m.ap[:, 0:n], src, row.ap[:, 0:n], ALU.mult), t_row, m.free)
            a = S.put(lambda e: e.activation(m.ap[:, 0:n], m.ap[:, 0:n], ACT.Identity, scale=gain,
                                             bias=0.0 if shift is None else shift), a, t_gain)
            t = split(m.ap[:, 0:n], hi, lo, a, free, eng=V)
            m.free = t
            row.free = t
            return t

        tA = [None] * 16
        tC = [None] * 16
        for k in range(16):
            tA[k] = modulated(k, H[:, k, NM:L], rx, t_rx, T, AH[:, k, 0:T], AL[:, k, 0:T],
                              vt[:, G1 + k:G1 + k + 1], modv[:, k:k + 1], [t_g1, t_m])
            tC[k] = modulated(k, ctxv[:, k, :], rc, t_rc, T, CH[:, k, :], CL[:, k, :],
                              vt[:, G1C + k:G1C + k + 1], modv[:, 96 + k:97 + k], [t_g1c, t_m])

        lat = lambda k: [(AH[:, k, 0:T], AL[:, k, 0:T], slice(0, T))]
        both = lambda k: [(AH[:, k, 0:T], AL[:, k, 0:T], slice(0, T)), (CH[:, k, :], CL[:, k, :], slice(T, 2 * T))]

        KA = G16[:, :].rearrange("p (m t) -> p m t", m=8)
        vf = Ring([sb(f"vf{i}", [128, 512], F32, early, "right") for i in range(2)])
        tK, tVt = [None] * 8, [None] * 8

        def k_out(m, b, p):
            tK[m] = S.put(lambda e: e.activation(KA[:, m, :], b.ap[:, :], ACT.Identity, bias=col("b_in", 40 + m)),
                          p, tC[15])
            b.free = [tK[m]]
            yield

        def v_out(m, b, p):
            f = vf.get()
            t = S.put(lambda e: e.activation(f.ap[:, :], b.ap[:, :], ACT.Identity, bias=col("b_in", 48 + m)), p, f.free)
            b.free = [t]
            yield
            for j in range(4):
                q = PE.put(lambda e, j=j: e.transpose(TB.ap[:, 128 * j:128 * j + 128], f.ap[:, 128 * j:128 * j + 128],
                                                      ident), t, TB.free, t_cst)
            f.free = [q]
            tVt[m] = V.put(lambda e: e.tensor_copy(VTok[:, :, 128 * m:128 * m + 128],
                                                   TB.ap[:, :].rearrange("p (j c) -> p j c", j=4)), q)
            TB.free = [tVt[m]]
            yield

        for m in range(16):
            b, p = gemm("w_in", 40 + m, (0, 1), both, lambda k: [tA[k], tC[k]], 2 * T)
            spawn(k_out(m, b, p) if m < 8 else v_out(m - 8, b, p))
        finish(*active)
        pe_kv = p
        early.close()

        Q = sb("Q", [128, 8, T], F32, phase)
        Bt = Ring([sb(f"Bt{i}", [128, 6, 64], F32, phase) for i in range(3)])
        Pt = Ring([sb(f"Pt{i}", [128, 512], F32, phase) for i in range(3)])
        PT = Ring([sb(f"PT{i}", [128, 4, T], F32, phase) for i in range(2)])
        mid = ExitStack()
        NA, SGV = sb("NA", [128, 8, T], F32, mid, "right"), sb("SGV", [128, 8, T], F32, mid, "right")
        tQ, tB, tNA = [None] * 8, {}, [None] * 8
        rel = ar["rpb"]
        Sb = Ring([])
        Sb.bufs = [S0, S1]
        b_sem = [sem(f"s_bt{i}") for i in range(3)]

        def by_row(ap):
            return ap.rearrange("p (r c) -> p r c", r=4)

        def turned(ap):
            return by_row(ap)[:, :, ::-1]

        def load_bias(h):
            bt = Bt.get()
            for half in range(2):
                src = bass.AP(rel.tensor, rel.offset + (h * 15 + 5 - half) * 128, [[1, 64], [128, 6], [1, 64]])
                SP.put(lambda e, half=half, src=src: e.dma_start(bt.ap[64 * half:64 * half + 64, :, :], src),
                       bt.free, pe_kv, mark=False, inc=(b_sem[h % 3], 16))
            t = (b_sem[h % 3], 32 * (h // 3 + 1))
            mask = cst[:, C_MASK:C_MASK + 64].unsqueeze(1).broadcast_to([128, 6, 64])
            a = G.put(lambda e: e.tensor_tensor(bt.ap[:, :, :], bt.ap[:, :, :], mask, ALU.add), t, t_cst)
            tB[h] = (bt, a)

        def attend(h, qt):
            m, r0 = h // 2, 64 * (h % 2)
            rs = slice(r0, r0 + 64)
            bt, t_b = tB[h]
            s = Sb.get()
            p = PE.put(lambda e: e.matmul(s.ap[:, :], Q[rs, m, 128 * qt:128 * qt + 128], KA[rs, m, :],
                                          start=True, stop=True), tQ[m], tK[m], s.free)
            j0 = 2 - 2 * qt
            loc = s.ap[:, 0:T].rearrange("p (r c) -> p r c", r=4)
            sc = st4.get()
            a = V.put(lambda e: e.tensor_tensor(loc, loc, bt.ap[:, j0:j0 + 4, :], ALU.add), p, t_b)
            if qt:
                bt.free = [a]
            a = V.put(lambda e: e.reduce_max(sc.ap[:, 0:1], s.ap[:, :], AX.X, negate=True), a, sc.free)
            pb = Pt.get()
            x = S.put(lambda e: e.activation(pb.ap[:, :], s.ap[:, :], ACT.Exp, bias=sc.ap[:, 0:1],
                                             accum_out=sc.ap[:, 1:2]), a, pb.free)
            s.free = [x]
            yield
            a = V.put(lambda e: e.reciprocal(sc.ap[:, 2:3], sc.ap[:, 1:2]), x)
            a = V.put(lambda e: e.tensor_scalar(pb.ap[:, :], pb.ap[:, :], sc.ap[:, 2:3], None, ALU.mult), a)
            sc.free = [a]
            yield
            for j in range(4):
                q = PE.put(lambda e, j=j: e.transpose(TB.ap[:, 128 * j:128 * j + 128],
                                                      pb.ap[:, 128 * j:128 * j + 128], ident), a, TB.free)
            pb.free = [q]
            if qt == 0:
                bufs[h] = PT.get()
            pt_buf = bufs[h]
            dst = pt_buf.ap[:, :, 128 * qt:128 * qt + 128]
            src = TB.ap[:, :].rearrange("p (j c) -> p j c", j=4)
            if qt:
                t = V.put(lambda e: e.tensor_copy(dst, src), q, pt_buf.free)
            else:
                t = S.put(lambda e: e.activation(dst, src, ACT.Copy), q, pt_buf.free)
            TB.free = [t]
            pt_tok.setdefault(h, []).append(t)
            yield
            if not qt:
                return
            for j in range(4):
                q = PE.put(lambda e, j=j: e.matmul(XB.ap[rs, 0:T], VTok[:, j, 64 * h:64 * h + 64], pt_buf.ap[:, j, :],
                                                   start=(j == 0), stop=(j == 3)), pt_tok[h], tVt[m], XB.free)
            pt_buf.free = [q]
            tNA[m] = V.put(lambda e: e.tensor_copy(turned(NA[rs, m, :]), by_row(XB.ap[rs, 0:T])), q)
            XB.free = [tNA[m]]
            yield

        pt_tok, bufs = {}, {}
        for h in range(3):
            load_bias(h)

        def q_out(m, b, p):
            tQ[m] = S.put(lambda e: e.activation(turned(Q[:, m, :]), by_row(b.ap[:, 0:T]), ACT.Identity, scale=0.125,
                                                 bias=vt[:, BQ + m:BQ + m + 1]), p, t_bq, pe_kv)
            b.free = [tQ[m]]
            yield

        def gelu2(dst, b, p, bias, free=()):
            x, u = tmp.get(), tmp.get()
            n = T
            a = S.put(lambda e: e.activation(x.ap[:, 0:n], b.ap[:, 0:n], ACT.Identity, bias=bias), p, x.free)
            c = S.put(lambda e: e.activation(u.ap[:, 0:n], b.ap[:, 0:n], ACT.Square, bias=bias), u.free)
            b.free = [c]
            yield
            d = V.put(lambda e: e.tensor_scalar(u.ap[:, 0:n], u.ap[:, 0:n], 0.044715, 1.0, ALU.mult, ALU.add), c)
            d = V.put(lambda e: e.tensor_tensor(u.ap[:, 0:n], u.ap[:, 0:n], x.ap[:, 0:n], ALU.mult), d, a)
            yield
            c = S.put(lambda e: e.activation(u.ap[:, 0:n], u.ap[:, 0:n], ACT.Tanh, scale=0.7978845608028654), d)
            yield
            d = V.put(lambda e: e.scalar_tensor_tensor(out=dst, in0=u.ap[:, 0:n], scalar=1.0, in1=x.ap[:, 0:n],
                                                       op0=ALU.add, op1=ALU.mult), c, *free)
            x.free = [d]
            u.free = [d]
            yield
            return d

        tSG = [None] * 8

        def sgv_out(m, b, p):
            d = yield from gelu2(SGV[:, m, :], b, p, col("b_in", 24 + m), free=(pe_kv,))
            tSG[m] = V.put(lambda e: e.tensor_scalar(SGV[:, m, :], SGV[:, m, :], 0.5, None, ALU.mult), d)

        nxt = [0]

        def feed():
            u = nxt[0]
            if u < 32 and tQ[(u // 2) // 2] is not None:
                h, qt = u // 2, u % 2
                if qt == 1 and 1 <= h < 14:
                    load_bias(h + 2)
                spawn(attend(h, qt))
                nxt[0] += 1

        def feeder():
            while nxt[0] < 32:
                feed()
                yield

        fd = spawn(feeder())
        for m in range(8):
            b, p = gemm("w_in", 32 + m, (0, 1), lat, lambda k: [], T)
            spawn(q_out(m, b, p))
        for m in range(8):
            b, p = gemm("w_in", 24 + m, (0, 1), lat, lambda k: [], T)
            spawn(sgv_out(m, b, p))
        finish(fd)
        finish(*active)
        t_att = [tNA[7], (PE.sem, PE.count), (S.sem, S.count), (V.sem, V.count), (G.sem, G.count)]

        def layer_norm(src, t_src, done):
            for m in range(8):
                t = add_up(m == 0, src[:, m, :], t_src(m), T)
                if m % 2:
                    yield
            mean = rows.get()
            p = PE.put(lambda e: e.matmul(XB.ap[:, 0:T], onesD[1024][:, :], ssum.ap[:, 0:T], start=True, stop=True),
                       t, XB.free)
            ssum.free = [p]
            a = S.put(lambda e: e.activation(mean.ap[:, 0:T], XB.ap[:, 0:T], ACT.Copy), p, mean.free)
            XB.free = [a]
            yield
            for m in range(8):
                c = V.put(lambda e, m=m: e.tensor_tensor(src[:, m, :], src[:, m, :], mean.ap[:, 0:T], ALU.subtract), a, t)
                _, q = square_up(m == 0, src[:, m, :], c, T)
                if m % 2:
                    yield
            mean.free = [c]
            done.append(inv_root(1024, T, q))
            yield

        VN = SGV
        tVN = [None] * 8

        def sgv_norm():
            done = []
            yield from layer_norm(SGV, lambda m: tSG[m], done)
            r, t = done[0]
            for m in range(8):
                a = V.put(lambda e, m=m: e.tensor_tensor(SGV[:, m, :], SGV[:, m, :], r.ap[:, 0:T], ALU.mult), t)
                tVN[m] = S.put(lambda e, m=m: e.activation(VN[:, m, :], SGV[:, m, :], ACT.Identity,
                                                           scale=col("sln_g", m), bias=col("sln_b", m)), a, t_att)
                if m % 2:
                    yield
            r.free = [a]

        sn = spawn(sgv_norm())
        phase.close()
        brs = ExitStack()
        BH, BL = sb("BH", [128, 8, T], F32R, brs), sb("BL", [128, 8, T], F32R, brs)
        tg = Ring([sb(f"tg{i}", [128, T], F32, brs) for i in range(3)])
        U = sb("U", [128, 8, T + 30], F32, mid, "right")
        CV = sb("CV", [128, 8, T], F32, mid, "right")
        t_pad = V.put(lambda e: e.memset(U[:, :, 0:15], 0.0), t_att)
        t_pad = V.put(lambda e: e.memset(U[:, :, T + 15:T + 30], 0.0))
        tU, tCV = [None] * 8, [None] * 8
        a1b = {}

        def glu_out(m, b, p):
            b1 = a1b.pop(m)
            x, g = tmp.get(), tmp.get()
            a = S.put(lambda e: e.activation(x.ap[:, 0:T], b1[0].ap[:, 0:T], ACT.Identity, bias=col("b_in", m)),
                      b1[1], x.free)
            b1[0].free = [a]
            c = S.put(lambda e: e.activation(g.ap[:, 0:T], b.ap[:, 0:T], ACT.Tanh, scale=0.5,
                                             bias=vt[:, HB + 8 + m:HB + 9 + m]), p, g.free, t_hb)
            b.free = [c]
            yield
            tU[m] = V.put(lambda e: e.scalar_tensor_tensor(out=U[:, m, 15:15 + T], in0=g.ap[:, 0:T], scalar=1.0,
                                                           in1=x.ap[:, 0:T], op0=ALU.add, op1=ALU.mult), c, t_att)
            x.free = [tU[m]]
            g.free = [tU[m]]
            yield

        def convolve():
            n = 0
            for m in range(8):
                while tU[m] is None:
                    yield
                for w in range(31):
                    s = col("conv_w", 8 * w + m)
                    if w == 0:
                        t = V.put(lambda e, m=m, s=s: e.tensor_scalar(CV[:, m, :], U[:, m, 0:T], s, col("conv_b", m),
                                                                      ALU.mult, ALU.add), tU[m], t_pad, t_cw)
                    else:
                        t = V.put(lambda e, m=m, w=w, s=s: e.scalar_tensor_tensor(
                            out=CV[:, m, :], in0=U[:, m, w:w + T], scalar=s, in1=CV[:, m, :], op0=ALU.mult,
                            op1=ALU.add), t)
                    n += 1
                    if n % 3 == 0:
                        yield
                tCV[m] = t

        cv = None
        for m in range(8):
            a1b[m] = gemm("w_in", m, (0, 1), lat, lambda k: [], T)
            b, p = gemm("w_in", 8 + m, (0, 1), lat, lambda k: [], T)
            spawn(glu_out(m, b, p))
            if m == 0:
                finish(sn)
                cv = spawn(convolve())

        WS = G16[:, 0:1024].rearrange("p (g q) -> p g q", g=8)
        BSr = G16[:, 1024:2048].rearrange("p (g q) -> p g q", g=8)
        VQ = Ring([G16[:, 2048 + 256 * i:2304 + 256 * i].rearrange("p (c q) -> p c q", c=2) for i in range(4)])
        right = [(V.sem, V.count), (S.sem, S.count), (PE.sem, PE.count), (G.sem, G.count)]
        t_ws = load(WS[:, :, :], ar["sgu_w"], right)
        t_bs = load(BSr[:, :, :], ar["sgu_b"].partition_broadcast(128), right)
        tBr = [None] * 8

        def sgu_out(m, b, p):
            vq = VQ.get()
            for c in range(2):
                q = PE.put(lambda e, c=c: e.transpose(TB.ap[:, 128 * c:128 * c + 128], VN[:, m, 128 * c:128 * c + 128],
                                                      ident), tVN[m], TB.free)
            t = S.put(lambda e: e.activation(vq.ap[:, :, :], TB.ap[:, 0:T].rearrange("p (c q) -> p c q", c=2),
                                             ACT.Copy), q, vq.free, right)
            TB.free = [t]
            x = tmp.get()
            d = yield from gelu2(x.ap[:, 0:T], b, p, col("b_in", 16 + m), free=(x.free,))
            for c in range(2):
                q = PE.put(lambda e, c=c: e.matmul(XB.ap[:, 128 * c:128 * c + 128], vq.ap[:, c, :], WS[:, m, :],
                                                   start=True, stop=True), t, t_ws, XB.free)
            vq.free = [q]
            y = tmp.get()
            bs = BSr[:, m, :].unsqueeze(1).broadcast_to([128, 2, 128])
            a = V.put(lambda e: e.tensor_tensor(y.ap[:, 0:T].rearrange("p (c q) -> p c q", c=2),
                                                XB.ap[:, 0:T].rearrange("p (c q) -> p c q", c=2), bs, ALU.add),
                      q, y.free, t_bs)
            XB.free = [a]
            a = V.put(lambda e: e.tensor_tensor(y.ap[:, 0:T], y.ap[:, 0:T], x.ap[:, 0:T], ALU.mult), a, d)
            x.free = [a]
            yield
            tBr[m] = yield from split_later(y.ap[:, 0:T], BH[:, m, :], BL[:, m, :], a, (t_att,), scale=0.5)
            y.free = tBr[m]
            yield

        for m in range(8):
            b, p = gemm("w_in", 16 + m, (0, 1), lat, lambda k: [], T)
            spawn(sgu_out(m, b, p))
        while any(t is None for t in tBr):
            step()

        M = G16[:, :].rearrange("p (m t) -> p m t", m=16)
        br = lambda k: [(BH[:, k, :], BL[:, k, :], slice(0, T))]
        tM = [None] * 16
        tMX = [None] * 16
        mix = {}

        def gate_out(g0, m, b, p, box):
            g = tg.get()
            t = S.put(lambda e: e.activation(g.ap[:, :], b.ap[:, 0:T], ACT.Tanh, scale=0.5,
                                             bias=vt[:, HB + g0 + m:HB + g0 + m + 1]), p, g.free, t_hb, right)
            b.free = [t]
            box.append((g, t))
            yield

        def branch_out(n, m, b, p, box):
            g, t = box[0]
            free = []
            if n == 0:
                tM[m] = V.put(lambda e: e.scalar_tensor_tensor(out=M[:, m, :], in0=g.ap[:, :], scalar=1.0,
                                                               in1=b.ap[:, 0:T], op0=ALU.add, op1=ALU.mult),
                              p, t, tVN[7], (PE.sem, PE.count))
                b.free = [tM[m]]
                g.free = [tM[m]]
                yield
                return
            x = tmp.get()
            a = V.put(lambda e: e.scalar_tensor_tensor(out=x.ap[:, 0:T], in0=g.ap[:, :], scalar=1.0,
                                                       in1=b.ap[:, 0:T], op0=ALU.add, op1=ALU.mult), p, t, x.free)
            b.free = [a]
            g.free = [a]
            if n == 1:
                tM[m] = G.put(lambda e: e.tensor_tensor(M[:, m, :], M[:, m, :], x.ap[:, 0:T], ALU.add), a, tM[m])
                x.free = [tM[m]]
                yield
                return
            a = V.put(lambda e: e.tensor_tensor(x.ap[:, 0:T], x.ap[:, 0:T], M[:, m, :], ALU.add), a, tM[m])
            yield
            YH, YL = mix["t"]
            tMX[m] = yield from split_later(x.ap[:, 0:T], YH[:, m, 0:T], YL[:, m, 0:T], a, (mix["free"],), scale=0.5)
            x.free = tMX[m]
            yield

        def conv_norm():
            done = []
            yield from layer_norm(CV, lambda m: tCV[m], done)
            r, t = done[0]
            for m in range(8):
                y, z = tmp.get(), tmp.get()
                a = V.put(lambda e, m=m, y=y: e.tensor_tensor(y.ap[:, 0:T], CV[:, m, :], r.ap[:, 0:T], ALU.mult), t, y.free)
                a = S.put(lambda e, m=m, y=y: e.activation(y.ap[:, 0:T], y.ap[:, 0:T], ACT.Identity,
                                                           scale=col("cln_g", m), bias=col("cln_b", m)), a)
                c = S.put(lambda e, y=y, z=z: e.activation(z.ap[:, 0:T], y.ap[:, 0:T], ACT.Tanh, scale=0.5), a, z.free)
                a = V.put(lambda e, m=m, y=y, z=z: e.scalar_tensor_tensor(out=CV[:, m, :], in0=z.ap[:, 0:T], scalar=1.0,
                                                                in1=y.ap[:, 0:T], op0=ALU.add, op1=ALU.mult), c)
                y.free = [a]
                z.free = [a]
                tCV[m] = a
                yield
            r.free = [a]

        for n, (g0, name) in enumerate(((72, "w_sgu"), (88, "w_na"), (56, "w_conv"))):
            if n == 1:
                for k in range(8):
                    tBr[k] = split(NA[:, k, :], BH[:, k, :], BL[:, k, :], t_att, (p,), eng=V)
                finish(cv)
                cn = spawn(conv_norm())
            if n == 2:
                finish(cn)
                for k in range(8):
                    tBr[k] = split(CV[:, k, :], BH[:, k, :], BL[:, k, :], tCV[k], (p,), scale=0.5)
                mid.close()
                free_mid = [(V.sem, V.count), (S.sem, S.count), (G.sem, G.count)]
                mix["t"] = (sb("YH", [128, 16, L], F32R, ctx, "right"), sb("YL", [128, 16, L], F32R, ctx, "right"))
                mix["free"] = free_mid
            for m in range(16):
                box = []
                b, p = gemm("w_in", g0 + m, (0, 1), lat, lambda k: [], T)
                spawn(gate_out(g0, m, b, p, box))
                b, p = gemm(name, m, (0,), br, lambda k: tBr[k], T)
                while not box:
                    step()
                spawn(branch_out(n, m, b, p, box))
        YH, YL = mix["t"]
        while any(t is None for t in tMX):
            step()

        mixed = lambda k: [(YH[:, k, 0:T], YL[:, k, 0:T], slice(0, T))]
        tH = [None] * 16
        sq = {}

        def wo_out(m, b, p):
            x = tmp.get()
            a = S.put(lambda e: e.activation(x.ap[:, 0:T], b.ap[:, 0:T], ACT.Identity, bias=col("b_o", m)), p, x.free)
            b.free = [a]
            yield
            tH[m] = V.put(lambda e: e.scalar_tensor_tensor(out=H[:, m, NM:L], in0=x.ap[:, 0:T],
                                                           scalar=modv[:, 32 + m:33 + m], in1=H[:, m, NM:L],
                                                           op0=ALU.mult, op1=ALU.add), a, [t_modv[8 + m // 4]])
            x.free = [tH[m]]
            sq["t"] = square_up(m == 0, H[:, m, NM:L], tH[m], T)
            yield

        for m in range(16):
            b, p = gemm("w_o", m, (0, 1), mixed, lambda k: tMX[k], T)
            spawn(wo_out(m, b, p))
            pe_wo = p
        finish(*active)
        r, t_r = inv_root(2048, T, sq["t"][1])
        t_g2 = V.put(lambda e: e.scalar_tensor_tensor(out=vt[:, G2M:G2M + 16], in0=modv[:, 64:80], scalar=1.0,
                                                      in1=cols("n2g", 16), op0=ALU.add, op1=ALU.mult),
                     [t_modv[j] for j in range(12, 20)])
        for k in range(16):
            tA[k] = modulated(k, H[:, k, NM:L], r, t_r, T, AH[:, k, 0:T], AL[:, k, 0:T], vt[:, G2M + k:G2M + k + 1],
                              modv[:, 48 + k:49 + k], [t_g2], free=(pe_wo,))

        tF = [None] * 16

        def ff1_out(c, m, b, p, pe_old):
            x = tmp.get()
            a = S.put(lambda e: e.activation(x.ap[:, 0:T], b.ap[:, 0:T], ACT.Relu, bias=col("b_ff1", 16 * c + m)),
                      p, x.free)
            b.free = [a]
            yield
            a = V.put(lambda e: e.tensor_tensor(x.ap[:, 0:T], x.ap[:, 0:T], x.ap[:, 0:T], ALU.mult), a)
            yield
            tF[m] = yield from split_later(x.ap[:, 0:T], YH[:, m, 0:T], YL[:, m, 0:T], a, (pe_old,))
            x.free = tF[m]
            yield

        def ff2_out(c, m, b, p):
            g = modv[:, 80 + m:81 + m]
            if c < 3:
                tH[m] = V.put(lambda e: e.scalar_tensor_tensor(out=H[:, m, NM:L], in0=b.ap[:, 0:T], scalar=g,
                                                               in1=H[:, m, NM:L], op0=ALU.mult, op1=ALU.add),
                              p, [t_modv[20 + m // 4]], tH[m], tA[m])
                b.free = [tH[m]]
                yield
                return
            x = tmp.get()
            a = S.put(lambda e: e.activation(x.ap[:, 0:T], b.ap[:, 0:T], ACT.Identity, bias=col("b_ff2", m)), p, x.free)
            b.free = [a]
            yield
            tH[m] = V.put(lambda e: e.scalar_tensor_tensor(out=H[:, m, NM:L], in0=x.ap[:, 0:T], scalar=g,
                                                           in1=H[:, m, NM:L], op0=ALU.mult, op1=ALU.add), a, tH[m])
            x.free = [tH[m]]
            sq["t"] = square_up(m == 0, H[:, m, NM:L], tH[m], T)
            yield

        pe_old = pe_wo
        for c in range(4):
            for m in range(16):
                b, p = gemm("w_ff1", 16 * c + m, (0, 1), lat, lambda k: tA[k], T)
                spawn(ff1_out(c, m, b, p, pe_old))
            finish(*active)
            for m in range(16):
                b, p = gemm("w_ff2", m, (2 * c, 2 * c + 1), mixed, lambda k: tF[k], T)
                spawn(ff2_out(c, m, b, p))
            pe_old = p
        finish(*active)

        def pre_norm(i, r, t_r, free, n0=0):
            for k in range(16):
                tA[k] = modulated(k, H[:, k, 0:L], r, t_r, L, AH[:, k, 0:L], AL[:, k, 0:L], col("pre_g", 16 * i + k),
                                  None, [], free=free)

        r, t_r = inv_root(2048, T, sq["t"][1])
        for k in range(16):
            a = V.put(lambda e, k=k, r=r: e.tensor_tensor(H[:, k, NM:L], H[:, k, NM:L], r.ap[:, 0:T], ALU.mult), t_r)
            tH[k] = S.put(lambda e, k=k: e.activation(H[:, k, NM:L], H[:, k, NM:L], ACT.Copy, scale=col("fin_g", k)), a)
            sq["t"] = square_up(k == 0, H[:, k, :], [tH[k], t_meta], L)
        r.free = [a]
        r, t_r = inv_root(2048, L, sq["t"][1])
        pre_norm(0, r, t_r, (p,))

        full = lambda k: [(AH[:, k, :], AL[:, k, :], slice(0, L))]
        brs.close()
        late = ExitStack()
        QK = Ring([G16[:, 4 * L * i:4 * L * i + 4 * L].rearrange("p (j t) -> p j t", j=4) for i in range(2)])
        SW = Buf(sb("SW", [32, 4, L], F32, late))
        VF = Ring([sb(f"VF{i}", [128, 2, L], F32, late) for i in range(2)])
        VK = Ring([G16[:, 2176 + 768 * i:2944 + 768 * i].rearrange("p (j c) -> p j c", j=3) for i in range(2)])
        GS = Ring([sb(f"GS{i}", [128, 2, L], F32, late) for i in range(2)])
        EE = Ring([sb(f"EE{i}", [128, 2, L], F32, late) for i in range(2)])
        AA = Buf(sb("AA", [128, 432], F32, late))
        AT = Buf(G16[:, 3712:4096])
        AM = Buf(sb("AM", [16, L], F32, late))
        ON = Buf(sb("ON", [128, 2, L], F32, late))
        base = [(V.sem, V.count), (S.sem, S.count), (G.sem, G.count), (PE.sem, PE.count)]
        tY = [None] * 16
        cosb = cst[0:32, C_COS:C_COS + L].unsqueeze(1).broadcast_to([32, 4, L])
        sinb = cst[0:32, C_SIN:C_SIN + L].unsqueeze(1).broadcast_to([32, 4, L])
        SWAP = [(j + 16) % 32 for j in range(32)]

        def diff_head(h, box):
            qk, vf_, vk, gs = box["qk"], box["vf"], box["vk"], box["gs"]
            r32 = qk.ap[0:32, :, :]
            a = V.put(lambda e: e.stream_shuffle(SW.ap[:, :, :], r32, SWAP), box["t_qk"], SW.free, base)
            a = V.put(lambda e: e.tensor_tensor(SW.ap[:, :, :], SW.ap[:, :, :], sinb, ALU.mult), a)
            c = V.put(lambda e: e.tensor_tensor(r32, r32, cosb, ALU.mult), a)
            yield
            t_qk = V.put(lambda e: e.tensor_tensor(r32, r32, SW.ap[:, :, :], ALU.add), c, a)
            SW.free = [t_qk]
            for d in range(2):
                for j, c0 in ((1, 16), (2, 144)):
                    q = PE.put(lambda e, d=d, j=j, c0=c0: e.transpose(
                        TB.ap[:, 256 * (j - 1) + 128 * d:256 * (j - 1) + 128 * d + 128], vf_.ap[:, d, c0:c0 + 128],
                        ident), box["t_v"], TB.free)
            for d in range(2):
                q2 = PE.put(lambda e, d=d: e.matmul(XB.ap[0:16, 128 * d:128 * d + 128], vf_.ap[:, d, 0:16], ident,
                                                    start=True, stop=True), box["t_v"], XB.free)
            vf_.free = [q, q2]
            a = S.put(lambda e: e.activation(vk.ap[:, 1:3, :], TB.ap[:, :].rearrange("p (j c) -> p j c", j=2),
                                             ACT.Copy), q, vk.free, base)
            TB.free = [a]
            t_v = S.put(lambda e: e.activation(vk.ap[0:16, 0, :], XB.ap[0:16, 0:256], ACT.Copy), q2)
            XB.free = [t_v]
            yield
            t_aa = []
            at = 0
            aa_free = AA.free

            def tile(q0, nq, nk, at):
                ee = EE.get()
                sc = st4.get()
                x = []
                for s_, bank in ((0, S0), (1, S1)):
                    q = PE.put(lambda e, s_=s_, bank=bank: e.matmul(bank.ap[0:nq, 0:nk], qk.ap[:, s_, q0:q0 + nq],
                                                                    qk.ap[:, 2 + s_, 0:nk], start=True, stop=True),
                               t_qk, bank.free)
                    a = q
                    if nq == 128:
                        a = V.put(lambda e, bank=bank: e.memset(bank.ap[0:64, nk - 64:nk], NEG), q)
                    a = V.put(lambda e, bank=bank, s_=s_: e.reduce_max(sc.ap[0:nq, s_:s_ + 1], bank.ap[0:nq, 0:nk],
                                                                       AX.X, negate=True), a, sc.free)
                    a = V.put(lambda e, s_=s_: e.tensor_scalar(sc.ap[0:nq, s_:s_ + 1], sc.ap[0:nq, s_:s_ + 1], SCALE2,
                                                               None, ALU.mult), a)
                    a = S.put(lambda e, s_=s_, bank=bank: e.activation(
                        ee.ap[0:nq, s_, 0:nk], bank.ap[0:nq, 0:nk], ACT.Exp, scale=SCALE2, bias=sc.ap[0:nq, s_:s_ + 1],
                        accum_out=sc.ap[0:nq, 2 + s_:3 + s_]), a, ee.free, base)
                    bank.free = [a]
                    x.append(a)
                qk.free = [q]
                yield
                a = V.put(lambda e: e.reciprocal(sc.ap[0:nq, 2:4], sc.ap[0:nq, 2:4]), x)
                a = V.put(lambda e: e.tensor_tensor(sc.ap[0:nq, 3:4], sc.ap[0:nq, 3:4], vt[0:nq, LAMC:LAMC + 1],
                                                    ALU.mult), a, t_lam)
                a = V.put(lambda e: e.tensor_scalar(ee.ap[0:nq, 1, 0:nk], ee.ap[0:nq, 1, 0:nk], sc.ap[0:nq, 3:4], None,
                                                    ALU.mult), a)
                a = V.put(lambda e: e.scalar_tensor_tensor(
                    out=AA.ap[0:nq, at:at + nk], in0=ee.ap[0:nq, 0, 0:nk], scalar=sc.ap[0:nq, 2:3],
                    in1=ee.ap[0:nq, 1, 0:nk], op0=ALU.mult, op1=ALU.subtract), a, aa_free, base)
                ee.free = [a]
                sc.free = [a]
                t_aa.append(a)
                yield

            for q0, nq, nk in ((144, 128, L), (16, 128, 144), (0, 16, 16)):
                yield from tile(q0, nq, nk, at)
                at += nk
            A2, A1, A0 = AA.ap[:, 0:L], AA.ap[:, L:L + 144], AA.ap[0:16, L + 144:L + 160]
            for dst, src in ((0, A1[:, 16:144]), (128, A2[:, 16:144]), (256, A2[:, 144:L])):
                q = PE.put(lambda e, dst=dst, src=src: e.transpose(TB.ap[:, dst:dst + 128], src, ident), t_aa, TB.free)
            t_at = S.put(lambda e: e.activation(AT.ap[:, :], TB.ap[:, 0:384], ACT.Copy), q, AT.free, base)
            TB.free = [t_at]
            for c0, n, src in ((0, 16, A0), (16, 128, A1[:, 0:16]), (144, 128, A2[:, 0:16])):
                q = PE.put(lambda e, c0=c0, n=n, src=src: e.matmul(XB.ap[0:16, c0:c0 + n], src, ident[0:n, 0:n],
                                                                   start=True, stop=True), t_aa, XB.free)
            AA.free = [q]
            t_am = S.put(lambda e: e.activation(AM.ap[:, :], XB.ap[0:16, 0:L], ACT.Copy), q, AM.free, base)
            XB.free = [t_am]
            yield
            o = []
            for d, bank in ((0, S0), (1, S1)):
                ds = slice(128 * d, 128 * d + 128)
                PE.put(lambda e, bank=bank, ds=ds: e.matmul(bank.ap[:, 0:L], vk.ap[0:16, 0, ds], AM.ap[:, :],
                                                            start=True, stop=False, skip_group_check=True),
                       t_am, t_v, bank.free, mark=False)
                PE.put(lambda e, bank=bank, ds=ds: e.matmul(bank.ap[:, NM:L], vk.ap[:, 1, ds], AT.ap[:, 0:T],
                                                            start=False, stop=False, skip_group_check=True),
                       t_at, mark=False)
                q = PE.put(lambda e, bank=bank, ds=ds: e.matmul(bank.ap[:, 144:L], vk.ap[:, 2, ds], AT.ap[:, T:384],
                                                                start=False, stop=True, skip_group_check=True))
                o.append(q)
                a = S.put(lambda e, d=d, bank=bank: e.activation(ON.ap[:, d, :], bank.ap[:, 0:L], ACT.Copy), q,
                          ON.free, base)
                bank.free = [a]
                _, t = square_up(d == 0, ON.ap[:, d, :], a, L)
            vk.free = [q]
            AT.free = [q]
            AM.free = [q]
            yield
            r, t_r = inv_root(256, L, t)
            yield
            for d in range(2):
                a = V.put(lambda e, d=d: e.tensor_tensor(ON.ap[:, d, :], ON.ap[:, d, :], r.ap[:, 0:L], ALU.mult), t_r)
                a = V.put(lambda e, d=d: e.scalar_tensor_tensor(out=ON.ap[:, d, :], in0=ON.ap[:, d, :],
                                                                scalar=vt[:, SG + d:SG + d + 1], in1=gs.ap[:, d, :],
                                                                op0=ALU.mult, op1=ALU.mult), a, t_sg, box["t_g"])
                tY[2 * h + d] = split(ON.ap[:, d, :], YH[:, 2 * h + d, :], YL[:, 2 * h + d, :], a, (pe_old,))
            r.free = [a]
            gs.free = [a]
            ON.free = tY[2 * h + 1] + tY[2 * h]
            yield

        def copy_out(dst, b, p, n, free, box, key):
            t = S.put(lambda e: e.activation(dst, b.ap[:, 0:n], ACT.Copy), p, free, base)
            b.free = [t]
            box.setdefault(key, []).append(t)
            yield

        def silu2_out(dst, b, p, n, c0, free, box, key):
            x = tmp.get()
            a = S.put(lambda e: e.activation(x.ap[:, 0:n], b.ap[:, c0:c0 + n], ACT.Tanh, scale=0.5), p, x.free)
            yield
            t = V.put(lambda e: e.scalar_tensor_tensor(out=dst, in0=x.ap[:, 0:n], scalar=1.0, in1=b.ap[:, c0:c0 + n],
                                                       op0=ALU.add, op1=ALU.mult), a, free, base)
            x.free = [t]
            b.free = [t]
            box.setdefault(key, []).append(t)
            yield

        heads = deque()

        def head_runner():
            done = 0
            while done < 8:
                while not heads:
                    yield
                h, box = heads.popleft()
                yield from diff_head(h, box)
                done += 1

        hr = spawn(head_runner())
        for h in range(8):
            box = {"qk": QK.get(), "vf": VF.get(), "vk": VK.get(), "gs": GS.get()}
            for m, kind, j in ((16, "qk", 2), (17, "qk", 3), (0, "qk", 0), (1, "qk", 1), (32, "vf", 0), (33, "vf", 1),
                               (48, "gs", 0), (49, "gs", 1)):
                b, p = gemm("w_ain", m + 2 * h, (0, 1), full, lambda k: tA[k], L)
                buf = box[kind]
                if kind == "gs":
                    spawn(silu2_out(buf.ap[:, j, :], b, p, L, 0, buf.free, box, "t_g"))
                else:
                    spawn(copy_out(buf.ap[:, j, :], b, p, L, buf.free, box, "t_qk" if kind == "qk" else "t_v"))
                    if m == 33:
                        step()
                        heads.append((h, box))
        finish(hr)
        finish(*active)
        late.close()

        last = ExitStack()
        Z = sb("Z", [128, 16, L], F32, last)
        G2 = G16[:, :].rearrange("p (m t) -> p m t", m=16)
        base2 = [(V.sem, V.count), (S.sem, S.count), (G.sem, G.count), (PE.sem, PE.count)]
        tZ = [None] * 16

        def z_out(m, b, p, n, free):
            tZ[m] = S.put(lambda e: e.activation(Z[:, m, 0:n], b.ap[:, 0:n], ACT.Copy), p, free)
            b.free = [tZ[m]]
            yield
            sq["t"] = square_up(m == 0, Z[:, m, 0:n], tZ[m], n)
            yield

        yfull = lambda k: [(YH[:, k, :], YL[:, k, :], slice(0, L))]
        for m in range(16):
            b, p = gemm("w_aout", m, (0, 1), yfull, lambda k: tY[k], L)
            spawn(z_out(m, b, p, L, base2))
        pe_ao = p
        finish(*active)

        r, t_r = inv_root(2048, L, sq["t"][1])
        for k in range(16):
            a = V.put(lambda e, k=k, r=r: e.tensor_tensor(Z[:, k, :], Z[:, k, :], r.ap[:, 0:L], ALU.mult), t_r)
            tH[k] = V.put(lambda e, k=k: e.scalar_tensor_tensor(out=H[:, k, :], in0=Z[:, k, :],
                                                                scalar=col("post_g", k), in1=H[:, k, :],
                                                                op0=ALU.mult, op1=ALU.add), a)
            sq["t"] = square_up(k == 0, H[:, k, :], tH[k], L)
        r.free = [a]
        z_free = [tH[15], a]
        r, t_r = inv_root(2048, L, sq["t"][1])
        pre_norm(1, r, t_r, (pe_ao,))

        def pool_out(m, b, p):
            u = [tmp.get() for _ in range(2)]
            t = S.put(lambda e: e.activation(u[0].ap[:, :], b.ap[:, 0:L], ACT.Copy), p, u[0].free)
            b.free = [t]
            yield
            src, w = u[0].ap, 1
            x = tmp.get()
            for i in range(m // 4 + 1):
                dst = u[1].ap if i % 2 == 0 else x.ap
                lo = 2 * w - 1
                t = V.put(lambda e, dst=dst, src=src, w=w, lo=lo: e.tensor_tensor(
                    dst[:, lo:L], src[:, lo:L], src[:, lo - w:L - w], ALU.add), t, u[1].free if i == 0 else x.free)
                src = dst
                w *= 2
            t = V.put(lambda e, src=src, w=w: e.scalar_tensor_tensor(out=x.ap[:, NM:L], in0=src[:, NM:L],
                                                                     scalar=1.0 / w, in1=u[0].ap[:, NM:L],
                                                                     op0=ALU.mult, op1=ALU.subtract), t, x.free)
            u[0].free = [t]
            u[1].free = [t]
            tY[m] = yield from split_later(x.ap[:, NM:L], YH[:, m, 0:T], YL[:, m, 0:T], t, (pe_ao,))
            x.free = tY[m]
            yield

        for m in range(16):
            b, p = gemm("w_pin", m, (0, 1), full, lambda k: tA[k], L)
            spawn(pool_out(m, b, p))
        gbox = {}
        tail = lambda k: [(AH[:, k, NM:L], AL[:, k, NM:L], slice(0, T))]
        for m in range(16):
            b, p = gemm("w_pin", 16 + m, (0, 1), tail, lambda k: [], T)
            spawn(silu2_out(G2[:, m, :], b, p, T, 0, base2, gbox, "g"))
        pe_g = p

        def grp_out(m, b, p):
            x = tmp.get()
            a = V.put(lambda e: e.scalar_tensor_tensor(out=x.ap[:, 0:T], in0=b.ap[:, 0:T],
                                                       scalar=vt[:, PB + m:PB + m + 1], in1=G2[:, m, :],
                                                       op0=ALU.mult, op1=ALU.mult), p, x.free, gbox["g"][m:m + 1], t_ps)
            b.free = [a]
            yield
            tA[m] = yield from split_later(x.ap[:, 0:T], AH[:, m, 0:T], AL[:, m, 0:T], a, (pe_g,))
            x.free = tA[m]
            yield

        while len(gbox["g"]) < 16:
            step()
        for g in range(4):
            for mp in range(2):
                s, t_hi, t_lo = use(("w_grp", g, mp))
                for mi in range(2):
                    b = acc.get()
                    for k in range(4):
                        kt = 4 * g + k
                        for q, (w, x, t) in enumerate(((his[s], YH, t_hi), (his[s], YL, None), (los[s], YH, t_lo))):
                            p = PE.put(lambda e, b=b, w=w, x=x, k=k, kt=kt, mi=mi, q=q: e.matmul(
                                b.ap[:, 0:T], w[:, 4 * mi + k, :], x[:, kt, 0:T], start=(k == 0 and q == 0),
                                stop=(k == 3 and q == 2)), t, tY[kt], b.free, mark=(k == 3 and q == 2))
                    spawn(grp_out(4 * g + 2 * mp + mi, b, p))
                split_free[s] = [p]
                step()
        while tA[15] is None or active:
            step()

        for m in range(16):
            b, p = gemm("w_pout", m, (0, 1), lat, lambda k: tA[k], T)
            spawn(z_out(m, b, p, T, z_free))
        finish(*active)
        r, t_r = inv_root(2048, T, sq["t"][1])
        s_out = sem("s_out")
        n_out = 0
        for k in range(16):
            a = V.put(lambda e, k=k, r=r: e.tensor_tensor(Z[:, k, 0:T], Z[:, k, 0:T], r.ap[:, 0:T], ALU.mult), t_r)
            a = V.put(lambda e, k=k: e.scalar_tensor_tensor(out=Z[:, k, 0:T], in0=Z[:, k, 0:T],
                                                            scalar=col("post_g", 16 + k), in1=H[:, k, NM:L],
                                                            op0=ALU.mult, op1=ALU.add), a)
            if k % 4 == 3:
                SP.put(lambda e, k=k: e.dma_start(out_d[:, k - 3:k + 1, :], Z[:, k - 3:k + 1, 0:T]), a, mark=False,
                       inc=(s_out, 16))
                n_out += 16
        last.close()
        assert st["use"] == len(plan)

        block = ctx.enter_context(nc.Block())

        @block.sync
        def _(eng):
            SP.run(eng)
            eng.wait_ge(s_out, n_out)

        @block.tensor
        def _(eng):
            PE.run(eng)

        @block.vector
        def _(eng):
            V.run(eng)

        @block.scalar
        def _(eng):
            S.run(eng)

        @block.gpsimd
        def _(eng):
            G.run(eng)


def _columns(v):
    return np.ascontiguousarray(v).reshape(-1, 128).T


def _units(w):
    k, m = w.shape
    return w.reshape(k // 1024, KU, 128, m // 128, 128).transpose(3, 0, 2, 1, 4).reshape(m // 128, k // 1024, 128, 1024)


def _tokens(x):
    return x.T.reshape(-1, 128, x.shape[0]).transpose(1, 0, 2)


def _constants():
    c = np.zeros((128, NCONST), np.float32)
    c[:, C_ID:C_ID + 128] = np.eye(128, dtype=np.float32)
    q = np.arange(64)
    start = np.clip(q - 8, 0, 48)[:, None]
    off = q[None, :] - start
    mask = np.where((off >= 0) & (off < 16), 0.0, NEG).astype(np.float32)
    c[:, C_MASK:C_MASK + 64] = np.concatenate([mask[::-1], mask[::-1]], 0)
    inv = np.float32(500000.0) ** (-np.arange(0, 32, 2, dtype=np.float32) / np.float32(32))
    ang = np.arange(L, dtype=np.float32)[:, None] * inv[None, :]
    cos, sin = np.cos(ang).T, np.sin(ang).T
    c[0:32, C_COS:C_COS + L] = np.concatenate([cos, cos], 0)
    c[0:32, C_SIN:C_SIN + L] = np.concatenate([-sin, sin], 0)
    c[:, C_ONE] = 1.0
    c[:, C_EPS] = EPS
    return c


def laid_out(inputs):
    a = {k: np.asarray(v) for k, v in inputs.items()}
    parts = {
        "c": a["c"], "cc": a["c_ctx"], "b_mod": a["b_mod"], "n1g": a["norm1_g"], "n2g": a["norm2_g"],
        "b_in": a["b_in"], "conv_b": a["conv_b"], "cln_g": a["conv_ln_g"], "cln_b": a["conv_ln_b"],
        "conv_w": a["conv_w"], "sln_g": a["sgu_ln_g"], "sln_b": a["sgu_ln_b"], "b_o": a["b_o"],
        "b_ff1": a["b_ff1"], "b_ff2": a["b_ff2"], "fin_g": a["final_g"], "pre_g": a["pre_norm_g_2"],
        "post_g": a["post_norm_g_2"], "sub_g": a["attn_subln_g_2"], "p_scale": a["pool_scale_2"],
        "lam": np.concatenate([a["attn_lambda_q1_2"], a["attn_lambda_q2_2"], a["attn_lambda_k1_2"],
                               a["attn_lambda_k2_2"]], 0),
    }
    vec = np.concatenate([_columns(parts[n]) for n, _ in VECS], 1)
    rpb = np.zeros((16, 15, 128), np.float32)
    rpb[:, :, 48:79] = a["na_rpb"][0]
    arrays = {
        "vec": vec,
        "cst": _constants(),
        "x": _tokens(a["x"][0]),
        "ctx": _tokens(a["ctx"][0]),
        "meta": _tokens(a["meta_tokens_2"]),
        "rpb": rpb,
        "sgu_w": a["sgu_w"][0].transpose(2, 0, 1),
        "sgu_b": a["sgu_b"][0],
        "w_mod": a["w_mod"][0].reshape(8, 2, 128, 24, 512).transpose(3, 0, 2, 1, 4).reshape(24, 8, 128, 1024),
        "w_grp": a["pool_w_group_2"][0].reshape(4, 4, 128, 2, 2, 128).transpose(0, 3, 2, 4, 1, 5)
        .reshape(4, 2, 128, 1024),
    }
    for name, src in (("w_in", "w_in"), ("w_sgu", "w_sgu_out"), ("w_na", "w_na_out"), ("w_conv", "w_conv_out"),
                      ("w_o", "w_o"), ("w_ff1", "w_ff1"), ("w_ff2", "w_ff2"), ("w_ain", "attn_w_in_2"),
                      ("w_aout", "attn_w_out_2"), ("w_pin", "pool_w_in_2"), ("w_pout", "pool_w_out_2")):
        arrays[name] = _units(a[src][0])
    return {name: np.ascontiguousarray(v) for name, v in arrays.items()}


def kernel(**inputs):
    import concourse.bacc as _bacc
    from concourse.bass_utils import run_bass_kernel_spmd as _run

    arrays = laid_out(inputs)
    nc = _bacc.Bacc("TRN2", target_bir_lowering=False, num_devices=1)
    aps, feed = {}, {}
    for name, v in arrays.items():
        feed[f"in_{name}"] = v
        aps[name] = nc.dram_tensor(f"in_{name}", v.shape, F32, kind="ExternalInput").ap()
    out = nc.dram_tensor("out_0", (128, 16, T), F32, kind="ExternalOutput").ap()
    build(nc, aps, out)
    r = _run(nc, [feed], core_ids=[0])
    got = np.asarray(r.results[0]["out_0"])
    return np.ascontiguousarray(got.transpose(2, 1, 0).reshape(1, T, D))
```

```python
from collections import deque
from contextlib import ExitStack

import numpy as np

import concourse.bass as bass
from concourse import mybir

F32 = mybir.dt.float32
F32R = mybir.dt.float32r
ALU = mybir.AluOpType
ACT = mybir.ActivationFunctionType
AX = mybir.AxisListType

D = 2048
T = 256
NM = 16
L = T + NM
KU = 8
NRAW = 4
NSPLIT = 5
AHEAD = 3
MOD_PE, MOD_DVE = (0, 4, 1, 5, 3, 7), (2, 6)
EPS = 1e-6
SCALE2 = 128.0 ** -0.5
NEG = -1e30

VECS = [("c", 16), ("cc", 16), ("b_mod", 96), ("n1g", 16), ("n2g", 16), ("b_in", 104), ("conv_b", 8),
        ("cln_g", 8), ("cln_b", 8), ("conv_w", 248), ("sln_g", 8), ("sln_b", 8), ("b_o", 16),
        ("b_ff1", 64), ("b_ff2", 16), ("fin_g", 16), ("pre_g", 32), ("post_g", 32), ("sub_g", 2),
        ("p_scale", 16), ("lam", 4)]
VOFF = {}
_at = 0
for _n, _w in VECS:
    VOFF[_n] = _at
    _at += _w
NVEC = _at
C_ID, C_MASK, C_COS, C_SIN, C_ONE, C_EPS = 0, 128, 192, 192 + L, 192 + 2 * L, 193 + 2 * L
NCONST = 194 + 2 * L


class Engine:

    def __init__(self, sem):
        self.sem, self.count, self.items, self.seen = sem, 0, [], {}

    def put(self, fn, *after, mark=True, inc=None):
        waits = []
        for t in flat(after):
            sem, v = t
            if self.seen.get(id(sem), 0) < v:
                self.seen[id(sem)] = v
                waits.append(t)
        if inc is None and mark:
            self.count += 1
            inc = (self.sem, 1)
        self.items.append((waits, fn, inc))
        return (self.sem, self.count) if mark else None

    def run(self, eng):
        for waits, fn, inc in self.items:
            for sem, v in waits:
                eng.wait_ge(sem, v)
            ins = fn(eng)
            if inc is not None:
                ins.then_inc(*inc)


def flat(x):
    for t in x:
        if t is None:
            continue
        if isinstance(t, list):
            yield from flat(t)
        else:
            yield t


class Buf:

    def __init__(self, ap):
        self.ap, self.after, self.held = ap, [], False

    @property
    def free(self):
        return self.after

    @free.setter
    def free(self, after):
        self.after, self.held = after, False


class Ring:
    def __init__(self, aps):
        self.bufs, self.n = [Buf(a) for a in aps], 0

    def get(self):
        for _ in self.bufs:
            b = self.bufs[self.n % len(self.bufs)]
            self.n += 1
            if not b.held:
                b.held = True
                return b
        raise ValueError("all of a ring's buffers are held")


def unit_plan():
    plan = []

    def full(name, m, kh=2):
        for h in range(kh):
            plan.append((name, m, h))

    def lead(name, m, h0=0):
        for h in range(2):
            for j in range(4):
                plan.append((name, m + j, h0 + h))

    mod = deque(("mod", nb, q) for nb in range(8, 24) for q in range(8))
    on_pe = deque(("mod0", nb, q) for nb in MOD_PE for q in range(8))
    on_dve = deque(("mod0", nb, q) for nb in MOD_DVE for q in range(8))
    for i in range(64):
        plan.append((on_dve if on_dve and i % 8 in (1, 4, 6) else on_pe).popleft())
    for m in list(range(40, 56)) + list(range(32, 40)) + list(range(24, 32)):
        full("w_in", m)
    for m in range(8):
        full("w_in", m)
        full("w_in", 8 + m)
    for m in range(16, 24):
        full("w_in", m)
    for g0, name in ((72, "w_sgu"), (88, "w_na"), (56, "w_conv")):
        for m in range(16):
            full("w_in", g0 + m)
            full(name, m, 1)
    for m in range(16):
        full("w_o", m)
    for c in range(4):
        if c == 0:
            lead("w_ff1", 0)
        for m in range(4 if c == 0 else 0, 16):
            full("w_ff1", 16 * c + m)
        lead("w_ff2", 0, 2 * c)
        for m in range(4, 16):
            plan.append(("w_ff2", m, 2 * c))
            plan.append(("w_ff2", m, 2 * c + 1))
    out = []
    for i, u in enumerate(plan):
        out.append(u)
        for _ in range(1 + i % 2 if 64 <= i < 96 else 1 if i >= 176 and i % 5 < 2 + (i % 10 == 9) else 0):
            if mod:
                out.append(mod.popleft())
    assert not mod and out.index(("mod", 19, 7)) < out.index(("w_conv", 14, 0))
    plan = out
    for h in range(8):
        for m in (16 + 2 * h, 17 + 2 * h, 2 * h, 2 * h + 1, 32 + 2 * h, 33 + 2 * h, 48 + 2 * h, 49 + 2 * h):
            full("w_ain", m)
    lead("w_aout", 0)
    for m in range(4, 16):
        full("w_aout", m)
    lead("w_pin", 0)
    for m in range(4, 32):
        full("w_pin", m)
    for g in range(4):
        plan += [("w_grp", g, 0), ("w_grp", g, 1)]
    lead("w_pout", 0)
    for m in range(4, 16):
        full("w_pout", m)
    return plan


def build(nc, ar, out_d):
    ctx = ExitStack()
    with ctx:
        def sem(name):
            return ctx.enter_context(nc.semaphore(name))

        def sb(name, shape, dt=F32, stack=ctx, side="left"):
            return stack.enter_context(nc.sbuf_tensor(name, shape, dt, side=side))

        PE, V, S, G, SP = (Engine(sem(n)) for n in ("s_pe", "s_dve", "s_act", "s_pool", "s_sp"))

        vec = sb("vec", [128, NVEC])
        cst = sb("cst", [128, NCONST])
        modv = sb("modv", [128, 128])
        vt = sb("vt", [128, 256])
        H = sb("H", [128, 16, L])
        AH, AL = sb("AH", [128, 16, L], F32R), sb("AL", [128, 16, L], F32R)
        raws = [sb(f"raw{i}", [128, KU * 128]) for i in range(NRAW)]
        his = [sb(f"hi{i}", [128, KU, 128], F32R) for i in range(NSPLIT)]
        los = [sb(f"lo{i}", [128, KU, 128], F32R) for i in range(NSPLIT)]
        tmp = Ring([sb(f"tmp{i}", [128, L]) for i in range(7)])
        sqr = Ring([sb(f"sqr{i}", [128, L]) for i in range(2)])
        ssum = Buf(sb("ssum", [128, L]))
        rows = Ring([sb(f"row{i}", [128, L]) for i in range(2)])
        st4 = Ring([sb(f"st{i}", [128, 4]) for i in range(6)])
        onesD = {n: sb(f"ones{n}", [128, 128]) for n in (2048, 1024, 256)}

        banks = [Buf(ctx.enter_context(nc.psum_tensor(f"ps{i}", [128, 512], F32))) for i in range(8)]
        acc = Ring([])
        acc.bufs = banks[0:4]
        S0, S1, TB, XB = banks[4:8]

        ident = cst[:, C_ID:C_ID + 128]
        one = cst[:, C_ONE:C_ONE + 1]
        eps = cst[:, C_EPS:C_EPS + 1]

        def col(name, i, rows_=slice(0, 128)):
            o = VOFF[name] + i
            return vec[rows_, o:o + 1]

        def cols(name, n, at=0):
            o = VOFF[name] + at
            return vec[:, o:o + n]

        def load(dst, src, *after):
            s = sem(f"s_ld{len(loads)}")
            loads.append(s)
            SP.put(lambda e: e.dma_start(dst, src), *after, mark=False, inc=(s, 16))
            return (s, 16)

        loads = []
        t_vec = load(vec[:, :], ar["vec"])
        t_cst = load(cst[:, :], ar["cst"])

        plan = unit_plan()
        raw_sem = [sem(f"s_raw{i}") for i in range(NRAW)]
        raw_free = [[] for _ in range(NRAW)]
        split_free = [[] for _ in range(NSPLIT)]
        st = {"dma": 0, "split": 0, "use": 0, "nsplit": 0}
        split_of = {}

        def issue(n=1):
            for _ in range(n):
                i = st["dma"]
                if i >= len(plan):
                    return
                st["dma"] += 1
                name, m, h = plan[i]
                src = ar["w_mod"][m, h] if name in ("mod", "mod0") else ar[name][m, h]
                dst = raws[i % NRAW][:, :]
                SP.put(lambda e, d=dst, s=src: e.dma_start(d, s), raw_free[i % NRAW], mark=False,
                       inc=(raw_sem[i % NRAW], 16))

        def landed(i):
            return (raw_sem[i % NRAW], 16 * (i // NRAW + 1))

        issue(NRAW)
        t_x = load(H[:, :, NM:L], ar["x"])
        t_meta = load(H[:, :, 0:NM], ar["meta"])

        later = deque()

        def split_unit(i):
            s = st["nsplit"] % NSPLIT
            st["nsplit"] += 1
            r = raws[i % NRAW]
            src = r[:, :].rearrange("p (k m) -> p k m", k=KU)
            hi, lo = his[s], los[s]
            t_hi = S.put(lambda e: e.activation(hi[:, :, :], src, ACT.Copy), landed(i), split_free[s])
            free = split_free[s]

            def low():
                t_lo = V.put(lambda e: e.tensor_tensor(lo[:, :, :], src, hi[:, :, :].bitcast(F32), ALU.subtract),
                             landed(i), t_hi, free)
                raw_free[i % NRAW] = [t_lo, t_hi]
                issue()
                split_of[i] = (s, t_hi, t_lo)

            later.append(low)

        gemv = {}

        def advance(ahead):
            for _ in range(len(later)):
                later.popleft()()
            while st["split"] < len(plan) and st["split"] <= st["use"] + ahead:
                i = st["split"]
                name = plan[i][0]
                if name == "mod0":
                    return
                st["split"] += 1
                if name == "mod":
                    later.append(lambda i=i: mod_unit(i))
                else:
                    split_unit(i)

        def use(key):
            while plan[st["use"]][0] == "mod":
                st["use"] += 1
            i = st["use"]
            assert plan[i] == key, (plan[i], key)
            n_mod = sum(plan[j][0] == "mod" for j in range(i, min(i + AHEAD + 3, len(plan))))
            advance(AHEAD + min(n_mod, 2))
            st["use"] += 1
            while i not in split_of:
                later.popleft()()
            s, t_hi, t_lo = split_of.pop(i)
            return s, t_hi, t_lo

        active = []

        def spawn(gen):
            active.append(gen)
            return gen

        def step():
            for g in list(active):
                if next(g, StopIteration) is StopIteration:
                    active.remove(g)

        def finish(*gens):
            for g in gens:
                while g in active:
                    step()

        def unit(b, key, kts, rhs, ready, start, stop):
            s, t_hi, t_lo = use(key)
            tok = None
            for k, kt in enumerate(kts):
                parts = rhs(kt)
                for j, (xh, xl, o) in enumerate(parts):
                    w0 = [ready(kt)] if j == 0 else []
                    for q, (w, x, t) in enumerate(((his[s], xh, t_hi), (his[s], xl, None), (los[s], xh, t_lo))):
                        f = start and k == 0 and j == 0 and q == 0
                        z = stop and k == KU - 1 and q == 2
                        last = k == KU - 1 and j == len(parts) - 1 and q == 2
                        tok = PE.put(lambda e, o=o, w=w, x=x, k=k, f=f, z=z, n=len(parts):
                                     e.matmul(b.ap[:, o], w[:, k, :], x, start=f, stop=z, skip_group_check=n > 1),
                                     [t] if j == 0 else [], w0 if q == 0 else [], b.free if f else [],
                                     mark=last) or tok
            split_free[s] = [tok]
            step()
            return tok

        def gemm(name, m, halves, rhs, ready, n):
            while all(b.held for b in acc.bufs):
                step()
            b = acc.get()
            for i, h in enumerate(halves):
                tok = unit(b, (name, m, h), range(KU * i, KU * i + KU), rhs, ready, i == 0, i == len(halves) - 1)
            return b, tok

        def gemm_lead(name, ms, halves, rhs, ready, out):
            while any(b.held for b in acc.bufs):
                step()
            bs = [acc.get() for _ in ms]
            for i, h in enumerate(halves):
                for m, b in zip(ms, bs):
                    tok = unit(b, (name, m, h), range(KU * i, KU * i + KU), rhs, ready, i == 0, i == 1)
                    if i == 1:
                        spawn(out(m, b, tok))
            return tok

        def got(toks, k):
            while toks[k] is None:
                step()
            return toks[k]

        def split(src, hi, lo, after, free=(), scale=1.0, eng=None):
            if eng is V:
                th = V.put(lambda e: e.tensor_copy(hi, src), after, *free)
            else:
                th = S.put(lambda e: e.activation(hi, src, ACT.Copy, scale=scale), after, *free)
            if scale == 1.0:
                tl = V.put(lambda e: e.tensor_tensor(lo, src, hi.bitcast(F32), ALU.subtract), after, th, *free)
            else:
                tl = V.put(lambda e: e.scalar_tensor_tensor(out=lo, in0=src, scalar=scale, in1=hi.bitcast(F32),
                                                            op0=ALU.mult, op1=ALU.subtract), after, th, *free)
            return [th, tl]

        def split_later(src, hi, lo, after, free=(), scale=1.0):
            th = S.put(lambda e: e.activation(hi, src, ACT.Copy, scale=scale), after, *free)
            yield
            if scale == 1.0:
                tl = V.put(lambda e: e.tensor_tensor(lo, src, hi.bitcast(F32), ALU.subtract), after, th, *free)
            else:
                tl = V.put(lambda e: e.scalar_tensor_tensor(out=lo, in0=src, scalar=scale, in1=hi.bitcast(F32),
                                                            op0=ALU.mult, op1=ALU.subtract), after, th, *free)
            return [th, tl]

        def split_scaled(src, gain, hi, lo, after, free=()):
            th = S.put(lambda e: e.activation(hi, src, ACT.Identity, scale=gain), after, *free)
            yield
            tl = V.put(lambda e: e.scalar_tensor_tensor(out=lo, in0=src, scalar=gain, in1=hi.bitcast(F32),
                                                        op0=ALU.mult, op1=ALU.subtract), after, th, *free)
            return [th, tl]

        t_ones = [V.put(lambda e, n=n, o=o: e.memset(o[:, :], 1.0 / n)) for n, o in onesD.items()]
        SC, HB, BQ, G1, G1C, G2M, LAMC, SG, PB, FP = 0, 32, 136, 144, 160, 176, 192, 196, 200, 216
        scv = vt[:, SC:SC + 32].rearrange("p (k t) -> p t k", t=2)
        tm = tmp.get()
        a = S.put(lambda e: e.activation(tm.ap[:, 0:32], vec[:, 0:32], ACT.Tanh, scale=0.5), t_vec)
        a = V.put(lambda e: e.tensor_scalar(tm.ap[:, 32:64], tm.ap[:, 0:32], 1.0, 0.5, ALU.add, ALU.mult), a)
        t_sc = V.put(lambda e: e.tensor_tensor(scv, tm.ap[:, 32:64].rearrange("p (t k) -> p t k", t=2),
                                               vec[:, 0:32].rearrange("p (t k) -> p t k", t=2), ALU.mult), a, t_vec)
        tm.free = [t_sc]
        t_hb = V.put(lambda e: e.tensor_scalar(vt[:, HB:HB + 104], cols("b_in", 104), 0.5, None, ALU.mult), t_vec)
        t_bq = V.put(lambda e: e.tensor_scalar(vt[:, BQ:BQ + 8], cols("b_in", 8, 32), 0.125, None, ALU.mult), t_vec)
        t_cw = V.put(lambda e: e.tensor_scalar(cols("conv_w", 248), cols("conv_w", 248), 0.5, None, ALU.mult), t_vec)
        a = V.put(lambda e: e.tensor_tensor(vt[:, LAMC:LAMC + 2], cols("lam", 2), cols("lam", 2, 2), ALU.mult), t_vec)
        onesf = sb("onesf", [128, 128])
        t_of = V.put(lambda e: e.memset(onesf[:, :], 1.0))
        a = PE.put(lambda e: e.matmul(XB.ap[:, 0:2], onesf[:, :], vt[:, LAMC:LAMC + 2], start=True, stop=True), a, t_of)
        a = S.put(lambda e: e.activation(vt[:, LAMC + 2:LAMC + 4], XB.ap[:, 0:2], ACT.Exp), a)
        XB.free = [a]
        a = V.put(lambda e: e.tensor_tensor(vt[:, LAMC:LAMC + 1], vt[:, LAMC + 2:LAMC + 3], vt[:, LAMC + 3:LAMC + 4],
                                            ALU.subtract), a)
        t_lam = V.put(lambda e: e.tensor_scalar(vt[:, LAMC:LAMC + 1], vt[:, LAMC:LAMC + 1], 0.2, None, ALU.add), a)
        t_sg = V.put(lambda e: e.tensor_scalar(vt[:, SG:SG + 2], cols("sub_g", 2), 0.8, 0.5, ALU.mult, ALU.mult), t_vec)
        t_fp = V.put(lambda e: e.tensor_tensor(vt[:, FP:FP + 16], cols("fin_g", 16), cols("pre_g", 16), ALU.mult), t_vec)
        t_ps = V.put(lambda e: e.tensor_scalar(vt[:, PB:PB + 16], cols("p_scale", 16), 0.5, None, ALU.mult), t_vec)

        def add_up(first, src, after, n, total=ssum):
            dst = total.ap[:, L - n:L] if n == T else total.ap[:, 0:n]
            if first:
                t = G.put(lambda e: e.tensor_copy(dst, src), after, total.free)
            else:
                t = G.put(lambda e: e.tensor_tensor(dst, dst, src, ALU.add), after, (G.sem, G.count))
            return t

        def square_up(first, src, after, n, total=ssum, scale=1.0):
            q = sqr.get()
            a = S.put(lambda e: e.activation(q.ap[:, 0:n], src, ACT.Square, scale=scale), after, q.free)
            t = add_up(first, q.ap[:, 0:n], a, n, total)
            q.free = [t]
            return a, t

        def mean_of(d, n, after, total=ssum):
            src = total.ap[:, L - n:L] if n == T else total.ap[:, 0:n]
            p = PE.put(lambda e: e.matmul(XB.ap[:, 0:n], onesD[d][:, :], src, start=True, stop=True),
                       after, t_ones, XB.free)
            total.free = [p]
            return p

        def inv_root(d, n, after, r=None):
            r = rows.get() if r is None else r
            p = mean_of(d, n, after)
            a = S.put(lambda e: e.activation(r.ap[:, 0:n], XB.ap[:, 0:n], ACT.Sqrt, bias=eps), p, r.free, t_cst)
            XB.free = [a]
            t = V.put(lambda e: e.reciprocal(r.ap[:, 0:n], r.ap[:, 0:n]), a)
            return r, t

        macc = Ring([sb(f"macc{i}", [128, 512]) for i in range(2)])

        def mod_unit(i):
            _, nb, q = plan[i]
            if q == 0:
                gemv["buf"] = macc.get()
            m = gemv["buf"]
            r = raws[i % NRAW]
            tok = gemv.get("tok")
            for j in range(2):
                k = 2 * q + j
                w = r[:, 512 * j:512 * j + 512]
                s = vt[:, SC + 2 * k:SC + 2 * k + 1]
                if k == 0:
                    tok = V.put(lambda e, w=w, s=s: e.tensor_scalar(m.ap[:, :], w, s, None, ALU.mult), landed(i), m.free, t_sc)
                else:
                    tok = V.put(lambda e, w=w, s=s: e.scalar_tensor_tensor(
                        out=m.ap[:, :], in0=w, scalar=s, in1=m.ap[:, :], op0=ALU.mult, op1=ALU.add),
                        landed(i), tok)
            gemv["tok"] = tok
            raw_free[i % NRAW] = [tok]
            issue()
            if q == 7:
                spawn(mod_out(nb, m, tok))

        t_modv = {}

        def mod_out(nb, m, tok):
            yield
            for j in range(4):
                p = PE.put(lambda e, j=j: e.matmul(XB.ap[:, j:j + 1], m.ap[:, 128 * j:128 * j + 128], one,
                                                   start=True, stop=True), tok, XB.free, t_cst)
            m.free = [p]
            t = V.put(lambda e: e.tensor_tensor(modv[:, 4 * nb:4 * nb + 4], XB.ap[:, 0:4], cols("b_mod", 4, 4 * nb),
                                                ALU.add), p, t_vec)
            XB.free = [t]
            t_modv[nb] = t
            yield

        early = ExitStack()
        mrow = Ring([sb(f"mrow{i}", [2, 512], F32, early, "right") for i in range(2)])
        t_mod0 = {}

        def mod0_add(nb, p):
            pv = XB.ap[:, 0:8].rearrange("p (j t) -> p t j", t=2)
            a = V.put(lambda e: e.tensor_tensor(modv[:, 4 * nb:4 * nb + 4], pv[:, 0, :], cols("b_mod", 4, 4 * nb),
                                                ALU.add), p, t_vec)
            a = V.put(lambda e: e.tensor_tensor(modv[:, 96 + 4 * nb:100 + 4 * nb], pv[:, 1, :],
                                                cols("b_mod", 4, 4 * nb), ALU.add))
            XB.free = [a]
            t_mod0[nb] = a

        def mod0_pe(nb, b, p):
            r = mrow.get()
            t = S.put(lambda e: e.activation(r.ap[:, :], b.ap[0:2, :], ACT.Copy), p, r.free)
            b.free = [t]
            yield
            yield
            for j in range(4):
                p = PE.put(lambda e, j=j: e.matmul(XB.ap[:, 2 * j:2 * j + 2], r.ap[0:2, 128 * j:128 * j + 128],
                                                   ident[0:2, 0:2], start=True, stop=True), t, XB.free, t_cst)
            r.free = [p]
            mod0_add(nb, p)
            yield

        def mod0_dve(nb, m, t):
            yield
            yield
            for j in range(4):
                for v in range(2):
                    p = PE.put(lambda e, j=j, v=v: e.matmul(
                        XB.ap[:, 2 * j + v:2 * j + v + 1], m[v].ap[:, 128 * j:128 * j + 128], one, start=True,
                        stop=True), t, XB.free, t_cst)
            m[0].free = [p]
            m[1].free = [p]
            mod0_add(nb, p)
            yield

        phase = ExitStack()
        G16 = sb("G16", [128, 16 * T])
        ctxv = G16[:, :].rearrange("p (k t) -> p k t", k=16)
        CH, CL = (sb(n, [128, 16, T], F32R, early, "right") for n in ("CH", "CL"))
        VTok = sb("VTok", [128, 4, 1024], F32, phase)
        XS = VTok[:, :, :].rearrange("p a (b t) -> p (a b) t", t=T)
        t_ctx = load(ctxv, ar["ctx"])
        t_xs = {}

        def norms():
            for src, dst, t_in, key in ((H[:, :, NM:L], XS, t_x, "x"), (ctxv, ctxv, t_ctx, "ctx")):
                for k in range(16):
                    _, t = square_up(k == 0, src[:, k, :], t_in, T)
                    if k % 2:
                        yield
                r, t = inv_root(2048, T, t)
                yield
                for k in range(16):
                    t_xs[key, k] = V.put(lambda e, k=k, r=r, src=src, dst=dst: e.tensor_tensor(
                        dst[:, k, :], src[:, k, :], r.ap[:, 0:T], ALU.mult), t)
                    if k % 4 == 3:
                        yield
                r.free = [t_xs[key, 15]]

        tA = [None] * 16
        tC = [None] * 16

        def modulate():
            for g in (0, 2, 1, 3):
                while g not in t_mod0 or 4 + g not in t_mod0 or ("ctx", 15) not in t_xs:
                    yield
                t_m = [t_mod0[g], t_mod0[4 + g]]
                for o, at in ((G1, 16), (G1C, 112)):
                    t_g = V.put(lambda e, o=o, at=at, g=g: e.scalar_tensor_tensor(
                        out=vt[:, o + 4 * g:o + 4 * g + 4], in0=modv[:, at + 4 * g:at + 4 * g + 4], scalar=1.0,
                        in1=cols("n1g", 4, 4 * g), op0=ALU.add, op1=ALU.mult), t_m)
                for k in range(4 * g, 4 * g + 4):
                    for src, hi, lo, o, at, key, res in ((XS, AH, AL, G1, 0, "x", tA), (ctxv, CH, CL, G1C, 96, "ctx", tC)):
                        gain, shift = vt[:, o + k:o + k + 1], modv[:, at + k:at + k + 1]
                        m = tmp.get()
                        a = V.put(lambda e, m=m, src=src, k=k, gain=gain, shift=shift: e.tensor_scalar(
                            m.ap[:, 0:T], src[:, k, :], gain, shift, ALU.mult, ALU.add), t_xs[key, k], t_g, m.free)
                        c = S.put(lambda e, m=m, hi=hi, k=k: e.activation(hi[:, k, 0:T], m.ap[:, 0:T], ACT.Copy), a)
                        res[k] = (m, c)
                    yield
                    for hi, lo, res in ((AH, AL, tA), (CH, CL, tC)):
                        m, c = res[k]
                        b = V.put(lambda e, m=m, hi=hi, lo=lo, k=k: e.tensor_tensor(
                            lo[:, k, 0:T], m.ap[:, 0:T], hi[:, k, 0:T].bitcast(F32), ALU.subtract), c)
                        m.free = [b]
                        res[k] = [c, b]

        spawn(norms())
        mg = spawn(modulate())
        for i in range(64):
            _, nb, q = plan[i]
            assert st["use"] == i
            st["use"] = st["split"] = i + 1
            r = raws[i % NRAW]
            if nb in MOD_PE:
                if q == 0:
                    b = acc.get()
                for j in range(2):
                    k = 2 * q + j
                    p = PE.put(lambda e, b=b, r=r, j=j, k=k: e.matmul(
                        b.ap[0:2, :], vt[:, SC + 2 * k:SC + 2 * k + 2], r[:, 512 * j:512 * j + 512],
                        start=(k == 0), stop=(k == 15)), landed(i), t_sc, b.free, mark=(j == 1))
                raw_free[i % NRAW] = [p]
                if q == 7:
                    spawn(mod0_pe(nb, b, p))
            else:
                if q == 0:
                    while any(x.held for x in macc.bufs):
                        step()
                    mm, ta = [macc.get(), macc.get()], [None, None]
                for j in range(2):
                    k = 2 * q + j
                    for v in range(2):
                        w, s, m = r[:, 512 * j:512 * j + 512], vt[:, SC + 2 * k + v:SC + 2 * k + v + 1], mm[v]
                        if k == 0:
                            ta[v] = V.put(lambda e, w=w, s=s, m=m: e.tensor_scalar(
                                m.ap[:, :], w, s, None, ALU.mult), landed(i), m.free, t_sc)
                        else:
                            ta[v] = V.put(lambda e, w=w, s=s, m=m: e.scalar_tensor_tensor(
                                out=m.ap[:, :], in0=w, scalar=s, in1=m.ap[:, :], op0=ALU.mult, op1=ALU.add),
                                landed(i), ta[v])
                raw_free[i % NRAW] = [ta[1]]
                if q == 7:
                    spawn(mod0_dve(nb, mm, ta[1]))
            issue()
            step()
        while any(x.held for x in macc.bufs):
            step()
        advance(AHEAD)
        finish(*active)

        lat = lambda k: [(AH[:, k, 0:T], AL[:, k, 0:T], slice(0, T))]
        both = lambda k: [(AH[:, k, 0:T], AL[:, k, 0:T], slice(0, T)), (CH[:, k, :], CL[:, k, :], slice(T, 2 * T))]

        KA = G16[:, :].rearrange("p (m t) -> p m t", m=8)
        vf = Ring([sb(f"vf{i}", [128, 512], F32, early, "right") for i in range(2)])
        tK, tVt = [None] * 8, [None] * 8

        def k_out(m, b, p):
            tK[m] = S.put(lambda e: e.activation(KA[:, m, :], b.ap[:, :], ACT.Identity, bias=col("b_in", 40 + m)),
                          p, tC[15])
            b.free = [tK[m]]
            yield

        def v_out(m, b, p):
            f = vf.get()
            t = S.put(lambda e: e.activation(f.ap[:, :], b.ap[:, :], ACT.Identity, bias=col("b_in", 48 + m)), p, f.free)
            b.free = [t]
            yield
            for j in range(4):
                q = PE.put(lambda e, j=j: e.transpose(TB.ap[:, 128 * j:128 * j + 128], f.ap[:, 128 * j:128 * j + 128],
                                                      ident), t, TB.free, t_cst)
            f.free = [q]
            tVt[m] = V.put(lambda e: e.tensor_copy(VTok[:, :, 128 * m:128 * m + 128],
                                                   TB.ap[:, :].rearrange("p (j c) -> p j c", j=4)), q, tA)
            TB.free = [tVt[m]]
            yield

        for m in range(16):
            b, p = gemm("w_in", 40 + m, (0, 1), both, lambda k: [tA[k], tC[k]], 2 * T)
            spawn(k_out(m, b, p) if m < 8 else v_out(m - 8, b, p))
        finish(*active)
        pe_kv = p
        early.close()

        Q = sb("Q", [128, 8, T], F32, phase)
        Bt = Ring([sb(f"Bt{i}", [128, 6, 64], F32, phase) for i in range(3)])
        Pt = Ring([sb(f"Pt{i}", [128, 512], F32, phase) for i in range(3)])
        PT = Ring([sb(f"PT{i}", [128, 4, T], F32, phase) for i in range(2)])
        mid = ExitStack()
        NA, SGV = sb("NA", [128, 8, T], F32, mid, "right"), sb("SGV", [128, 8, T], F32, mid, "right")
        tQ, tB, tNA = [None] * 8, {}, [None] * 8
        rel = ar["rpb"]
        Sb = Ring([])
        Sb.bufs = [S0, S1]
        b_sem = [sem(f"s_bt{i}") for i in range(3)]

        def by_row(ap):
            return ap.rearrange("p (r c) -> p r c", r=4)

        def turned(ap):
            return by_row(ap)[:, :, ::-1]

        def load_bias(h):
            bt = Bt.get()
            for half in range(2):
                src = bass.AP(rel.tensor, rel.offset + (h * 15 + 5 - half) * 128, [[1, 64], [128, 6], [1, 64]])
                SP.put(lambda e, half=half, src=src: e.dma_start(bt.ap[64 * half:64 * half + 64, :, :], src),
                       bt.free, pe_kv, mark=False, inc=(b_sem[h % 3], 16))
            t = (b_sem[h % 3], 32 * (h // 3 + 1))
            mask = cst[:, C_MASK:C_MASK + 64].unsqueeze(1).broadcast_to([128, 6, 64])
            a = G.put(lambda e: e.tensor_tensor(bt.ap[:, :, :], bt.ap[:, :, :], mask, ALU.add), t, t_cst)
            tB[h] = (bt, a)

        def attend(h, qt):
            m, r0 = h // 2, 64 * (h % 2)
            rs = slice(r0, r0 + 64)
            bt, t_b = tB[h]
            s = Sb.get()
            p = PE.put(lambda e: e.matmul(s.ap[:, :], Q[rs, m, 128 * qt:128 * qt + 128], KA[rs, m, :],
                                          start=True, stop=True), tQ[m], tK[m], s.free)
            j0 = 2 - 2 * qt
            loc = s.ap[:, 0:T].rearrange("p (r c) -> p r c", r=4)
            sc = st4.get()
            a = V.put(lambda e: e.tensor_tensor(loc, loc, bt.ap[:, j0:j0 + 4, :], ALU.add), p, t_b)
            if qt:
                bt.free = [a]
            a = V.put(lambda e: e.reduce_max(sc.ap[:, 0:1], s.ap[:, :], AX.X, negate=True), a, sc.free)
            pb = Pt.get()
            x = S.put(lambda e: e.activation(pb.ap[:, :], s.ap[:, :], ACT.Exp, bias=sc.ap[:, 0:1],
                                             accum_out=sc.ap[:, 1:2]), a, pb.free)
            s.free = [x]
            yield
            a = V.put(lambda e: e.reciprocal(sc.ap[:, 2:3], sc.ap[:, 1:2]), x)
            a = V.put(lambda e: e.tensor_scalar(pb.ap[:, :], pb.ap[:, :], sc.ap[:, 2:3], None, ALU.mult), a)
            sc.free = [a]
            yield
            for j in range(4):
                q = PE.put(lambda e, j=j: e.transpose(TB.ap[:, 128 * j:128 * j + 128],
                                                      pb.ap[:, 128 * j:128 * j + 128], ident), a, TB.free)
            pb.free = [q]
            if qt == 0:
                bufs[h] = PT.get()
            pt_buf = bufs[h]
            dst = pt_buf.ap[:, :, 128 * qt:128 * qt + 128]
            src = TB.ap[:, :].rearrange("p (j c) -> p j c", j=4)
            if qt:
                t = V.put(lambda e: e.tensor_copy(dst, src), q, pt_buf.free)
            else:
                t = S.put(lambda e: e.activation(dst, src, ACT.Copy), q, pt_buf.free)
            TB.free = [t]
            pt_tok.setdefault(h, []).append(t)
            yield
            if not qt:
                return
            for j in range(4):
                q = PE.put(lambda e, j=j: e.matmul(XB.ap[rs, 0:T], VTok[:, j, 64 * h:64 * h + 64], pt_buf.ap[:, j, :],
                                                   start=(j == 0), stop=(j == 3)), pt_tok[h], tVt[m], XB.free)
            pt_buf.free = [q]
            tNA[m] = V.put(lambda e: e.tensor_copy(turned(NA[rs, m, :]), by_row(XB.ap[rs, 0:T])), q)
            XB.free = [tNA[m]]
            yield

        pt_tok, bufs = {}, {}
        for h in range(3):
            load_bias(h)

        def q_out(m, b, p):
            tQ[m] = S.put(lambda e: e.activation(turned(Q[:, m, :]), by_row(b.ap[:, 0:T]), ACT.Identity, scale=0.125,
                                                 bias=vt[:, BQ + m:BQ + m + 1]), p, t_bq, pe_kv)
            b.free = [tQ[m]]
            yield

        def gelu2(dst, b, p, bias, free=()):
            x, u = tmp.get(), tmp.get()
            n = T
            a = S.put(lambda e: e.activation(x.ap[:, 0:n], b.ap[:, 0:n], ACT.Identity, bias=bias), p, x.free)
            c = S.put(lambda e: e.activation(u.ap[:, 0:n], b.ap[:, 0:n], ACT.Square, bias=bias), u.free)
            b.free = [c]
            yield
            d = V.put(lambda e: e.tensor_scalar(u.ap[:, 0:n], u.ap[:, 0:n], 0.044715, 1.0, ALU.mult, ALU.add), c)
            d = V.put(lambda e: e.tensor_tensor(u.ap[:, 0:n], u.ap[:, 0:n], x.ap[:, 0:n], ALU.mult), d, a)
            yield
            c = S.put(lambda e: e.activation(u.ap[:, 0:n], u.ap[:, 0:n], ACT.Tanh, scale=0.7978845608028654), d)
            yield
            d = V.put(lambda e: e.scalar_tensor_tensor(out=dst, in0=u.ap[:, 0:n], scalar=1.0, in1=x.ap[:, 0:n],
                                                       op0=ALU.add, op1=ALU.mult), c, *free)
            x.free = [d]
            u.free = [d]
            yield
            return d

        tSG = [None] * 8

        def sgv_out(m, b, p):
            d = yield from gelu2(SGV[:, m, :], b, p, col("b_in", 24 + m), free=(pe_kv,))
            tSG[m] = V.put(lambda e: e.tensor_scalar(SGV[:, m, :], SGV[:, m, :], 0.5, None, ALU.mult), d)

        nxt = [0]

        def feed():
            u = nxt[0]
            if u < 32 and tQ[(u // 2) // 2] is not None:
                h, qt = u // 2, u % 2
                if qt == 1 and 1 <= h < 14:
                    load_bias(h + 2)
                spawn(attend(h, qt))
                nxt[0] += 1

        def feeder():
            while nxt[0] < 32:
                feed()
                yield

        fd = spawn(feeder())
        for m in range(8):
            b, p = gemm("w_in", 32 + m, (0, 1), lat, lambda k: [], T)
            spawn(q_out(m, b, p))
        for m in range(8):
            b, p = gemm("w_in", 24 + m, (0, 1), lat, lambda k: [], T)
            spawn(sgv_out(m, b, p))
        a1b = {0: gemm("w_in", 0, (0, 1), lat, lambda k: [], T)}
        g1b = {0: gemm("w_in", 8, (0, 1), lat, lambda k: [], T)}
        a1b[1] = gemm("w_in", 1, (0, 1), lat, lambda k: [], T)
        finish(fd)
        finish(*active)
        t_att = [tNA[7], (PE.sem, PE.count), (S.sem, S.count), (V.sem, V.count), (G.sem, G.count)]

        def layer_norm(src, t_src, done):
            for m in range(8):
                t = add_up(m == 0, src[:, m, :], t_src(m), T)
                if m % 2:
                    yield
            mean = rows.get()
            p = mean_of(1024, T, t)
            a = S.put(lambda e: e.activation(mean.ap[:, 0:T], XB.ap[:, 0:T], ACT.Copy), p, mean.free)
            XB.free = [a]
            yield
            for m in range(8):
                c = V.put(lambda e, m=m: e.tensor_tensor(src[:, m, :], src[:, m, :], mean.ap[:, 0:T], ALU.subtract), a, t)
                _, q = square_up(m == 0, src[:, m, :], c, T)
                if m % 2:
                    yield
            mean.free = [c]
            done.append(inv_root(1024, T, q))
            yield

        VN = SGV
        tVN = [None] * 8

        def sgv_norm():
            done = []
            yield from layer_norm(SGV, lambda m: tSG[m], done)
            r, t = done[0]
            for m in range(8):
                a = V.put(lambda e, m=m: e.tensor_tensor(SGV[:, m, :], SGV[:, m, :], r.ap[:, 0:T], ALU.mult), t)
                tVN[m] = S.put(lambda e, m=m: e.activation(VN[:, m, :], SGV[:, m, :], ACT.Identity,
                                                           scale=col("sln_g", m), bias=col("sln_b", m)), a, t_att)
                if m % 2:
                    yield
            r.free = [a]

        sn = spawn(sgv_norm())
        phase.close()
        brs = ExitStack()
        BH, BL = sb("BH", [128, 8, T], F32R, brs), sb("BL", [128, 8, T], F32R, brs)
        tg = Ring([sb(f"tg{i}", [128, T], F32, brs) for i in range(3)])
        U = sb("U", [128, 8, T + 30], F32, mid, "right")
        CV = sb("CV", [128, 8, T], F32, mid, "right")
        t_pad = V.put(lambda e: e.memset(U[:, :, 0:15], 0.0), t_att)
        t_pad = V.put(lambda e: e.memset(U[:, :, T + 15:T + 30], 0.0))
        tU, tCV = [None] * 8, [None] * 8

        def glu_out(m, b, p):
            b1 = a1b.pop(m)
            x, g = tmp.get(), tmp.get()
            a = S.put(lambda e: e.activation(x.ap[:, 0:T], b1[0].ap[:, 0:T], ACT.Identity, bias=col("b_in", m)),
                      b1[1], x.free)
            b1[0].free = [a]
            c = S.put(lambda e: e.activation(g.ap[:, 0:T], b.ap[:, 0:T], ACT.Tanh, scale=0.5,
                                             bias=vt[:, HB + 8 + m:HB + 9 + m]), p, g.free, t_hb)
            b.free = [c]
            yield
            tU[m] = V.put(lambda e: e.scalar_tensor_tensor(out=U[:, m, 15:15 + T], in0=g.ap[:, 0:T], scalar=1.0,
                                                           in1=x.ap[:, 0:T], op0=ALU.add, op1=ALU.mult), c, t_att)
            x.free = [tU[m]]
            g.free = [tU[m]]
            yield

        def convolve():
            n = 0
            for m in range(8):
                while tU[m] is None:
                    yield
                for w in range(31):
                    s = col("conv_w", 8 * w + m)
                    if w == 0:
                        t = V.put(lambda e, m=m, s=s: e.tensor_scalar(CV[:, m, :], U[:, m, 0:T], s, col("conv_b", m),
                                                                      ALU.mult, ALU.add), tU[m], t_pad, t_cw)
                    else:
                        t = V.put(lambda e, m=m, w=w, s=s: e.scalar_tensor_tensor(
                            out=CV[:, m, :], in0=U[:, m, w:w + T], scalar=s, in1=CV[:, m, :], op0=ALU.mult,
                            op1=ALU.add), t)
                    n += 1
                    if n % 2 == 0:
                        yield
                tCV[m] = t
            yield from conv_norm()

        def conv_norm():
            done = []
            yield from layer_norm(CV, lambda m: tCV[m], done)
            r, t = done[0]
            for m in range(8):
                y, z = tmp.get(), tmp.get()
                a = V.put(lambda e, m=m, y=y: e.tensor_tensor(y.ap[:, 0:T], CV[:, m, :], r.ap[:, 0:T], ALU.mult), t, y.free)
                a = S.put(lambda e, m=m, y=y: e.activation(y.ap[:, 0:T], y.ap[:, 0:T], ACT.Identity,
                                                           scale=col("cln_g", m), bias=col("cln_b", m)), a)
                c = S.put(lambda e, y=y, z=z: e.activation(z.ap[:, 0:T], y.ap[:, 0:T], ACT.Tanh, scale=0.5), a, z.free)
                a = V.put(lambda e, m=m, y=y, z=z: e.scalar_tensor_tensor(out=CV[:, m, :], in0=z.ap[:, 0:T], scalar=1.0,
                                                                in1=y.ap[:, 0:T], op0=ALU.add, op1=ALU.mult), c)
                y.free = [a]
                z.free = [a]
                tCV[m] = a
                yield
            r.free = [a]

        cv = None
        for m in range(8):
            if m > 1:
                a1b[m] = gemm("w_in", m, (0, 1), lat, lambda k: [], T)
            b, p = g1b[0] if m == 0 else gemm("w_in", 8 + m, (0, 1), lat, lambda k: [], T)
            spawn(glu_out(m, b, p))
            if m == 0:
                finish(sn)
                cv = spawn(convolve())

        WS = G16[:, 0:1024].rearrange("p (g q) -> p g q", g=8)
        BSr = G16[:, 1024:2048].rearrange("p (g q) -> p g q", g=8)
        VQ = Ring([G16[:, 2048 + 256 * i:2304 + 256 * i].rearrange("p (c q) -> p c q", c=2) for i in range(4)])
        right = [(V.sem, V.count), (S.sem, S.count), (PE.sem, PE.count), (G.sem, G.count)]
        t_ws = load(WS[:, :, :], ar["sgu_w"], right)
        t_bs = load(BSr[:, :, :], ar["sgu_b"].partition_broadcast(128), right)
        tBr = [None] * 8

        def sgu_out(m, b, p):
            vq = VQ.get()
            for c in range(2):
                q = PE.put(lambda e, c=c: e.transpose(TB.ap[:, 128 * c:128 * c + 128], VN[:, m, 128 * c:128 * c + 128],
                                                      ident), tVN[m], TB.free)
            t = S.put(lambda e: e.activation(vq.ap[:, :, :], TB.ap[:, 0:T].rearrange("p (c q) -> p c q", c=2),
                                             ACT.Copy), q, vq.free, right)
            TB.free = [t]
            x = tmp.get()
            d = yield from gelu2(x.ap[:, 0:T], b, p, col("b_in", 16 + m), free=(x.free,))
            for c in range(2):
                q = PE.put(lambda e, c=c: e.matmul(XB.ap[:, 128 * c:128 * c + 128], vq.ap[:, c, :], WS[:, m, :],
                                                   start=True, stop=True), t, t_ws, XB.free)
            vq.free = [q]
            y = tmp.get()
            bs = BSr[:, m, :].unsqueeze(1).broadcast_to([128, 2, 128])
            a = V.put(lambda e: e.tensor_tensor(y.ap[:, 0:T].rearrange("p (c q) -> p c q", c=2),
                                                XB.ap[:, 0:T].rearrange("p (c q) -> p c q", c=2), bs, ALU.add),
                      q, y.free, t_bs)
            XB.free = [a]
            a = V.put(lambda e: e.tensor_tensor(y.ap[:, 0:T], y.ap[:, 0:T], x.ap[:, 0:T], ALU.mult), a, d)
            x.free = [a]
            yield
            tBr[m] = yield from split_later(y.ap[:, 0:T], BH[:, m, :], BL[:, m, :], a, (t_att,), scale=0.5)
            y.free = tBr[m]
            yield

        for m in range(8):
            b, p = gemm("w_in", 16 + m, (0, 1), lat, lambda k: [], T)
            spawn(sgu_out(m, b, p))
        while any(t is None for t in tBr):
            step()

        M = G16[:, :].rearrange("p (m t) -> p m t", m=16)
        br = lambda k: [(BH[:, k, :], BL[:, k, :], slice(0, T))]
        tM = [None] * 16
        tMX = [None] * 16
        mix = {}

        def gate_out(g0, m, b, p, box):
            g = tg.get()
            t = S.put(lambda e: e.activation(g.ap[:, :], b.ap[:, 0:T], ACT.Tanh, scale=0.5,
                                             bias=vt[:, HB + g0 + m:HB + g0 + m + 1]), p, g.free, t_hb, right)
            b.free = [t]
            box.append((g, t))
            yield

        def branch_out(n, m, b, p, box):
            g, t = box[0]
            free = []
            if n == 0:
                tM[m] = V.put(lambda e: e.scalar_tensor_tensor(out=M[:, m, :], in0=g.ap[:, :], scalar=1.0,
                                                               in1=b.ap[:, 0:T], op0=ALU.add, op1=ALU.mult),
                              p, t, tVN[7], (PE.sem, PE.count))
                b.free = [tM[m]]
                g.free = [tM[m]]
                yield
                return
            x = tmp.get()
            a = V.put(lambda e: e.scalar_tensor_tensor(out=x.ap[:, 0:T], in0=g.ap[:, :], scalar=1.0,
                                                       in1=b.ap[:, 0:T], op0=ALU.add, op1=ALU.mult), p, t, x.free)
            b.free = [a]
            g.free = [a]
            if n == 1:
                tM[m] = G.put(lambda e: e.tensor_tensor(M[:, m, :], M[:, m, :], x.ap[:, 0:T], ALU.add), a, tM[m])
                x.free = [tM[m]]
                yield
                return
            a = V.put(lambda e: e.tensor_tensor(x.ap[:, 0:T], x.ap[:, 0:T], M[:, m, :], ALU.add), a, tM[m])
            yield
            YH, YL = mix["t"]
            tMX[m] = yield from split_later(x.ap[:, 0:T], YH[:, m, 0:T], YL[:, m, 0:T], a, (mix["free"],), scale=0.5)
            x.free = tMX[m]
            yield

        for n, (g0, name) in enumerate(((72, "w_sgu"), (88, "w_na"), (56, "w_conv"))):
            if n == 1:
                for k in range(8):
                    tBr[k] = split(NA[:, k, :], BH[:, k, :], BL[:, k, :], t_att, (p,), eng=V)
            if n == 2:
                finish(cv)
                for k in range(8):
                    tBr[k] = split(CV[:, k, :], BH[:, k, :], BL[:, k, :], tCV[k], (p,), scale=0.5)
                mid.close()
                free_mid = [(V.sem, V.count), (S.sem, S.count), (G.sem, G.count)]
                mix["t"] = (sb("YH", [128, 16, L], F32R, ctx, "right"), sb("YL", [128, 16, L], F32R, ctx, "right"))
                mix["free"] = free_mid
            for m in range(16):
                box = []
                b, p = gemm("w_in", g0 + m, (0, 1), lat, lambda k: [], T)
                spawn(gate_out(g0, m, b, p, box))
                b, p = gemm(name, m, (0,), br, lambda k: tBr[k], T)
                while not box:
                    step()
                spawn(branch_out(n, m, b, p, box))
        YH, YL = mix["t"]
        while any(t is None for t in tMX):
            step()

        brs.close()
        rown, ssum2 = Buf(sb("rown", [128, L])), Buf(sb("ssum2", [128, L]))
        rown.free = ssum2.free = [(V.sem, V.count), (S.sem, S.count), (PE.sem, PE.count), (G.sem, G.count)]
        t_g2 = V.put(lambda e: e.scalar_tensor_tensor(out=vt[:, G2M:G2M + 16], in0=modv[:, 64:80], scalar=1.0,
                                                      in1=cols("n2g", 16), op0=ALU.add, op1=ALU.mult),
                     [t_modv[j] for j in range(12, 20)])
        shift = modv[:, 48:64].unsqueeze(2).broadcast_to([128, 16, 2])
        tSh = split(shift, AH[:, :, T:T + 2], AL[:, :, T:T + 2], [t_modv[j] for j in range(12, 16)])
        mixed = lambda k: [(YH[:, k, 0:T], YL[:, k, 0:T], slice(0, T))]
        tH = [None] * 16
        sums = {}

        def wo_out(m, b, p):
            x = tmp.get()
            a = S.put(lambda e: e.activation(x.ap[:, 0:T], b.ap[:, 0:T], ACT.Identity, bias=col("b_o", m)), p, x.free)
            b.free = [a]
            yield
            tH[m] = V.put(lambda e: e.scalar_tensor_tensor(out=H[:, m, NM:L], in0=x.ap[:, 0:T],
                                                           scalar=modv[:, 32 + m:33 + m], in1=H[:, m, NM:L],
                                                           op0=ALU.mult, op1=ALU.add), a, [t_modv[8 + m // 4]])
            x.free = [tH[m]]
            a, t = square_up(m == 0, H[:, m, NM:L], tH[m], T)
            if m == 15:
                sums["n2"] = t
            ts = yield from split_scaled(H[:, m, NM:L], vt[:, G2M + m:G2M + m + 1], AH[:, m, 0:T], AL[:, m, 0:T],
                                         tH[m], (t_g2, pe_br))
            tA[m] = ts + [a]
            yield

        row_t = {}

        def row_of(key, n):
            while key not in sums:
                yield
            yield
            _, row_t[key] = inv_root(2048, n, sums[key], rown)
            yield

        pe_br = p
        tA[:] = [None] * 16
        for m in range(16):
            b, p = gemm("w_o", m, (0, 1), mixed, lambda k: tMX[k], T)
            spawn(wo_out(m, b, p))
            pe_wo = p
        spawn(row_of("n2", T))

        tF = [None] * 16

        def ff1_out(c, m, b, p, pe_old):
            while "n2" not in row_t:
                yield
            x, sc = tmp.get(), st4.get()
            a = V.put(lambda e: e.tensor_tensor(x.ap[:, 0:T], b.ap[:, 0:T], rown.ap[:, 0:T], ALU.mult), p, row_t["n2"],
                      x.free)
            rown.free = [a]
            d = V.put(lambda e: e.tensor_tensor(sc.ap[:, 0:1], b.ap[:, T:T + 1], col("b_ff1", 16 * c + m), ALU.add),
                      p, sc.free)
            b.free = [d]
            a = V.put(lambda e: e.tensor_scalar(x.ap[:, 0:T], x.ap[:, 0:T], sc.ap[:, 0:1], 0.0, ALU.add, ALU.max), a, d)
            sc.free = [a]
            yield
            a = S.put(lambda e: e.activation(x.ap[:, 0:T], x.ap[:, 0:T], ACT.Square), a)
            tF[m] = yield from split_later(x.ap[:, 0:T], YH[:, m, 0:T], YL[:, m, 0:T], a, (pe_old,))
            x.free = tF[m]
            yield

        def ff2_out(c, m, b, p):
            g = modv[:, 80 + m:81 + m]
            if c < 3:
                tH[m] = V.put(lambda e: e.scalar_tensor_tensor(out=H[:, m, NM:L], in0=b.ap[:, 0:T], scalar=g,
                                                               in1=H[:, m, NM:L], op0=ALU.mult, op1=ALU.add),
                              p, [t_modv[20 + m // 4]], tH[m], tA[m])
                b.free = [tH[m]]
                yield
                return
            x = tmp.get()
            a = S.put(lambda e: e.activation(x.ap[:, 0:T], b.ap[:, 0:T], ACT.Identity, bias=col("b_ff2", m)), p, x.free)
            b.free = [a]
            yield
            tH[m] = V.put(lambda e: e.scalar_tensor_tensor(out=H[:, m, NM:L], in0=x.ap[:, 0:T], scalar=g,
                                                           in1=H[:, m, NM:L], op0=ALU.mult, op1=ALU.add), a, tH[m])
            x.free = [tH[m]]
            yield
            th = S.put(lambda e: e.activation(AH[:, m, NM:L], H[:, m, NM:L], ACT.Identity, scale=vt[:, FP + m:FP + m + 1]),
                       tH[m], pe_ff1, t_fp)
            a, sums["s1"] = square_up(m == 0, H[:, m, NM:L], tH[m], T)
            a, sums["s2"] = square_up(m == 0, H[:, m, NM:L], tH[m], T, ssum2, col("fin_g", m))
            if m == 15:
                sums["ain"] = [sums["s2"], sums["meta"]]
            yield
            tl = V.put(lambda e: e.scalar_tensor_tensor(
                out=AL[:, m, NM:L], in0=H[:, m, NM:L], scalar=vt[:, FP + m:FP + m + 1], in1=AH[:, m, NM:L].bitcast(F32),
                op0=ALU.mult, op1=ALU.subtract), th, pe_ff1)
            tA[m] = [th, tl, a]
            yield

        def meta_tokens():
            m, q = tmp.get(), sqr.get()
            mv, qv = (z.ap[:, 0:T].rearrange("p (k t) -> p k t", k=16) for z in (m, q))
            src = H[:, :, 0:NM]
            a = V.put(lambda e: e.tensor_tensor(mv, src, cols("pre_g", 16).unsqueeze(2).broadcast_to([128, 16, NM]),
                                                ALU.mult), t_meta, t_vec, m.free)
            c = S.put(lambda e: e.activation(qv, src, ACT.Square), t_meta, q.free)
            yield
            t = V.put(lambda e: e.reduce_sum(ssum2.ap[:, 0:NM], qv.rearrange("p k t -> p t k"), AX.X), c, ssum2.free)
            q.free = [t]
            sums["meta"] = t
            ts = yield from split_later(mv, AH[:, :, 0:NM], AL[:, :, 0:NM], a, (pe_ff1,))
            m.free = ts
            sums["tm"] = ts
            yield

        pe_old = pe_wo
        shifted = lambda k: [(AH[:, k, 0:T + 2], AL[:, k, 0:T + 2], slice(0, T + 2))]
        for c in range(4):
            tF[:] = [None] * 16
            for m in range(16):
                if c == 0 and m < 4:
                    if m == 0:
                        gemm_lead("w_ff1", range(4), (0, 1), shifted, lambda k: [got(tA, k), tSh],
                                  lambda m, b, p: ff1_out(0, m, b, p, pe_wo))
                    continue
                b, p = gemm("w_ff1", 16 * c + m, (0, 1), shifted, lambda k: [tA[k], tSh], T + 2)
                spawn(ff1_out(c, m, b, p, pe_old))
            if c == 3:
                pe_ff1 = p
                tA[:] = [None] * 16
                spawn(meta_tokens())
            halves = (2 * c, 2 * c + 1)
            gemm_lead("w_ff2", range(4), halves, mixed, lambda k: got(tF, k), lambda m, b, p, c=c: ff2_out(c, m, b, p))
            for m in range(4, 16):
                b, p = gemm("w_ff2", m, halves, mixed, lambda k: tF[k], T)
                spawn(ff2_out(c, m, b, p))
            pe_old = p

        def last_norm():
            while "ain" not in sums:
                yield
            yield
            s1, t_s1 = inv_root(2048, T, sums["s1"])
            p2 = mean_of(2048, L, sums["ain"], ssum2)
            y = tmp.get()
            a = V.put(lambda e: e.tensor_tensor(y.ap[:, NM:L], XB.ap[:, NM:L], s1.ap[:, 0:T], ALU.mult), p2, t_s1, y.free)
            a = V.put(lambda e: e.tensor_tensor(y.ap[:, NM:L], y.ap[:, NM:L], s1.ap[:, 0:T], ALU.mult), a)
            c = V.put(lambda e: e.tensor_copy(y.ap[:, 0:NM], XB.ap[:, 0:NM]), p2)
            XB.free = [c]
            yield
            a = S.put(lambda e: e.activation(rown.ap[:, :], y.ap[:, :], ACT.Sqrt, bias=eps), a, c, rown.free)
            y.free = [a]
            a = V.put(lambda e: e.reciprocal(rown.ap[:, :], rown.ap[:, :]), a)
            row_t["ain"] = V.put(lambda e: e.tensor_tensor(rown.ap[:, NM:L], rown.ap[:, NM:L], s1.ap[:, 0:T], ALU.mult), a)
            yield
            for k in range(16):
                tH[k] = V.put(lambda e, k=k: e.scalar_tensor_tensor(
                    out=H[:, k, NM:L], in0=H[:, k, NM:L], scalar=col("fin_g", k), in1=s1.ap[:, 0:T], op0=ALU.mult,
                    op1=ALU.mult), t_s1, got(tA, k))
                if k % 2:
                    yield
            s1.free = [tH[15]]

        spawn(last_norm())

        full = lambda k: [(AH[:, k, :], AL[:, k, :], slice(0, L))]
        late = ExitStack()
        QK = Ring([G16[:, 4 * L * i:4 * L * i + 4 * L].rearrange("p (j t) -> p j t", j=4) for i in range(2)])
        SW = Buf(sb("SW", [32, 4, L], F32, late))
        VF = Ring([sb(f"VF{i}", [128, 2, L], F32, late) for i in range(2)])
        VK = Ring([G16[:, 2176 + 768 * i:2944 + 768 * i].rearrange("p (j c) -> p j c", j=3) for i in range(2)])
        GS = Ring([sb(f"GS{i}", [128, 2, L], F32, late) for i in range(2)])
        EE = Ring([sb(f"EE{i}", [128, 2, L], F32, late) for i in range(2)])
        AA = Buf(sb("AA", [128, 432], F32, late))
        AT = Buf(G16[:, 3712:4096])
        AM = Buf(sb("AM", [16, L], F32, late))
        ON = Buf(sb("ON", [128, 2, L], F32, late))
        base = [(V.sem, V.count), (S.sem, S.count), (G.sem, G.count), (PE.sem, PE.count)]
        tY = [None] * 16
        cosb = cst[0:32, C_COS:C_COS + L].unsqueeze(1).broadcast_to([32, 4, L])
        sinb = cst[0:32, C_SIN:C_SIN + L].unsqueeze(1).broadcast_to([32, 4, L])
        SWAP = [(j + 16) % 32 for j in range(32)]

        def diff_head(h, box):
            qk, vf_, vk, gs = box["qk"], box["vf"], box["vk"], box["gs"]
            r32 = qk.ap[0:32, :, :]
            a = V.put(lambda e: e.stream_shuffle(SW.ap[:, :, :], r32, SWAP), box["t_qk"], SW.free, base)
            a = V.put(lambda e: e.tensor_tensor(SW.ap[:, :, :], SW.ap[:, :, :], sinb, ALU.mult), a)
            c = V.put(lambda e: e.tensor_tensor(r32, r32, cosb, ALU.mult), a)
            yield
            t_qk = V.put(lambda e: e.tensor_tensor(r32, r32, SW.ap[:, :, :], ALU.add), c, a)
            SW.free = [t_qk]
            for d in range(2):
                for j, c0 in ((1, 16), (2, 144)):
                    q = PE.put(lambda e, d=d, j=j, c0=c0: e.transpose(
                        TB.ap[:, 256 * (j - 1) + 128 * d:256 * (j - 1) + 128 * d + 128], vf_.ap[:, d, c0:c0 + 128],
                        ident), box["t_v"], TB.free)
            for d in range(2):
                q2 = PE.put(lambda e, d=d: e.matmul(XB.ap[0:16, 128 * d:128 * d + 128], vf_.ap[:, d, 0:16], ident,
                                                    start=True, stop=True), box["t_v"], XB.free)
            vf_.free = [q, q2]
            swapped[h] = [t_qk, q, q2]
            a = S.put(lambda e: e.activation(vk.ap[:, 1:3, :], TB.ap[:, :].rearrange("p (j c) -> p j c", j=2),
                                             ACT.Copy), q, vk.free, base)
            TB.free = [a]
            t_v = S.put(lambda e: e.activation(vk.ap[0:16, 0, :], XB.ap[0:16, 0:256], ACT.Copy), q2)
            XB.free = [t_v]
            yield
            t_aa = []
            at = 0
            aa_free = AA.free

            def tile(q0, nq, nk, at):
                ee = EE.get()
                sc = st4.get()
                x = []
                for s_, bank in ((0, S0), (1, S1)):
                    q = PE.put(lambda e, s_=s_, bank=bank: e.matmul(bank.ap[0:nq, 0:nk], qk.ap[:, s_, q0:q0 + nq],
                                                                    qk.ap[:, 2 + s_, 0:nk], start=True, stop=True),
                               t_qk, bank.free)
                    a = q
                    if nq == 128:
                        a = V.put(lambda e, bank=bank: e.memset(bank.ap[0:64, nk - 64:nk], NEG), q)
                    a = V.put(lambda e, bank=bank, s_=s_: e.reduce_max(sc.ap[0:nq, s_:s_ + 1], bank.ap[0:nq, 0:nk],
                                                                       AX.X, negate=True), a, sc.free)
                    a = V.put(lambda e, s_=s_: e.tensor_scalar(sc.ap[0:nq, s_:s_ + 1], sc.ap[0:nq, s_:s_ + 1], SCALE2,
                                                               None, ALU.mult), a)
                    a = S.put(lambda e, s_=s_, bank=bank: e.activation(
                        ee.ap[0:nq, s_, 0:nk], bank.ap[0:nq, 0:nk], ACT.Exp, scale=SCALE2, bias=sc.ap[0:nq, s_:s_ + 1],
                        accum_out=sc.ap[0:nq, 2 + s_:3 + s_]), a, ee.free, base)
                    bank.free = [a]
                    x.append(a)
                qk.free = [q]
                yield
                a = V.put(lambda e: e.reciprocal(sc.ap[0:nq, 2:4], sc.ap[0:nq, 2:4]), x)
                a = V.put(lambda e: e.tensor_tensor(sc.ap[0:nq, 3:4], sc.ap[0:nq, 3:4], vt[0:nq, LAMC:LAMC + 1],
                                                    ALU.mult), a, t_lam)
                a = V.put(lambda e: e.tensor_scalar(ee.ap[0:nq, 1, 0:nk], ee.ap[0:nq, 1, 0:nk], sc.ap[0:nq, 3:4], None,
                                                    ALU.mult), a)
                a = V.put(lambda e: e.scalar_tensor_tensor(
                    out=AA.ap[0:nq, at:at + nk], in0=ee.ap[0:nq, 0, 0:nk], scalar=sc.ap[0:nq, 2:3],
                    in1=ee.ap[0:nq, 1, 0:nk], op0=ALU.mult, op1=ALU.subtract), a, aa_free, base)
                ee.free = [a]
                sc.free = [a]
                t_aa.append(a)
                yield

            for q0, nq, nk in ((144, 128, L), (16, 128, 144), (0, 16, 16)):
                yield from tile(q0, nq, nk, at)
                at += nk
            A2, A1, A0 = AA.ap[:, 0:L], AA.ap[:, L:L + 144], AA.ap[0:16, L + 144:L + 160]
            for dst, src in ((0, A1[:, 16:144]), (128, A2[:, 16:144]), (256, A2[:, 144:L])):
                q = PE.put(lambda e, dst=dst, src=src: e.transpose(TB.ap[:, dst:dst + 128], src, ident), t_aa, TB.free)
            t_at = S.put(lambda e: e.activation(AT.ap[:, :], TB.ap[:, 0:384], ACT.Copy), q, AT.free, base)
            TB.free = [t_at]
            for c0, n, src in ((0, 16, A0), (16, 128, A1[:, 0:16]), (144, 128, A2[:, 0:16])):
                q = PE.put(lambda e, c0=c0, n=n, src=src: e.matmul(XB.ap[0:16, c0:c0 + n], src, ident[0:n, 0:n],
                                                                   start=True, stop=True), t_aa, XB.free)
            AA.free = [q]
            t_am = S.put(lambda e: e.activation(AM.ap[:, :], XB.ap[0:16, 0:L], ACT.Copy), q, AM.free, base)
            XB.free = [t_am]
            yield
            o = []
            for d, bank in ((0, S0), (1, S1)):
                ds = slice(128 * d, 128 * d + 128)
                PE.put(lambda e, bank=bank, ds=ds: e.matmul(bank.ap[:, 0:L], vk.ap[0:16, 0, ds], AM.ap[:, :],
                                                            start=True, stop=False, skip_group_check=True),
                       t_am, t_v, bank.free, mark=False)
                PE.put(lambda e, bank=bank, ds=ds: e.matmul(bank.ap[:, NM:L], vk.ap[:, 1, ds], AT.ap[:, 0:T],
                                                            start=False, stop=False, skip_group_check=True),
                       t_at, mark=False)
                q = PE.put(lambda e, bank=bank, ds=ds: e.matmul(bank.ap[:, 144:L], vk.ap[:, 2, ds], AT.ap[:, T:384],
                                                                start=False, stop=True, skip_group_check=True))
                o.append(q)
                a = S.put(lambda e, d=d, bank=bank: e.activation(ON.ap[:, d, :], bank.ap[:, 0:L], ACT.Copy), q,
                          ON.free, base)
                bank.free = [a]
                _, t = square_up(d == 0, ON.ap[:, d, :], a, L)
            vk.free = [q]
            AT.free = [q]
            AM.free = [q]
            yield
            r, t_r = inv_root(256, L, t)
            yield
            for d in range(2):
                a = V.put(lambda e, d=d: e.tensor_tensor(ON.ap[:, d, :], ON.ap[:, d, :], r.ap[:, 0:L], ALU.mult), t_r)
                a = V.put(lambda e, d=d: e.scalar_tensor_tensor(out=ON.ap[:, d, :], in0=ON.ap[:, d, :],
                                                                scalar=vt[:, SG + d:SG + d + 1], in1=gs.ap[:, d, :],
                                                                op0=ALU.mult, op1=ALU.mult), a, t_sg, box["t_g"])
                tY[2 * h + d] = split(ON.ap[:, d, :], YH[:, 2 * h + d, :], YL[:, 2 * h + d, :], a, (pe_old,))
            r.free = [a]
            gs.free = [a]
            ON.free = tY[2 * h + 1] + tY[2 * h]
            yield

        def copy_out(dst, b, p, n, free, box, key):
            while "ain" not in row_t:
                yield
            t = V.put(lambda e: e.tensor_tensor(dst, b.ap[:, 0:n], rown.ap[:, 0:n], ALU.mult), p, row_t["ain"], free,
                      base)
            b.free = [t]
            rown.free = [t]
            box.setdefault(key, []).append(t)
            yield

        def silu2_out(dst, b, p, n, c0, free, box, key):
            while row_key[0] not in row_t:
                yield
            x, y = tmp.get(), tmp.get()
            c = V.put(lambda e: e.tensor_tensor(y.ap[:, 0:n], b.ap[:, 0:n], rown.ap[:, c0:c0 + n], ALU.mult), p,
                      row_t[row_key[0]], y.free)
            b.free = [c]
            rown.free = [c]
            yield
            a = S.put(lambda e: e.activation(x.ap[:, 0:n], y.ap[:, 0:n], ACT.Tanh, scale=0.5), c, x.free)
            yield
            t = V.put(lambda e: e.scalar_tensor_tensor(out=dst, in0=x.ap[:, 0:n], scalar=1.0, in1=y.ap[:, 0:n],
                                                       op0=ALU.add, op1=ALU.mult), a, free, base)
            x.free = [t]
            y.free = [t]
            box.setdefault(key, []).append(t)
            yield

        row_key = ["ain"]
        swapped = {}
        heads = deque()

        def head_runner():
            done = 0
            while done < 8:
                while not heads:
                    yield
                h, box = heads.popleft()
                yield from diff_head(h, box)
                done += 1

        hr = spawn(head_runner())
        for h in range(8):
            box = {"qk": QK.get(), "vf": VF.get(), "vk": VK.get(), "gs": GS.get()}
            for m, kind, j in ((16, "qk", 2), (17, "qk", 3), (0, "qk", 0), (1, "qk", 1), (32, "vf", 0), (33, "vf", 1),
                               (48, "gs", 0), (49, "gs", 1)):
                b, p = gemm("w_ain", m + 2 * h, (0, 1), full, lambda k: [got(tA, k), sums["tm"]], L)
                buf = box[kind]
                if kind == "gs":
                    spawn(silu2_out(buf.ap[:, j, :], b, p, L, 0, buf.free, box, "t_g"))
                else:
                    spawn(copy_out(buf.ap[:, j, :], b, p, L, buf.free, box, "t_qk" if kind == "qk" else "t_v"))
                    if m == 33:
                        while len(box.get("t_v", [])) < 2:
                            step()
                        heads.append((h, box))
        late.close()
        last = ExitStack()
        Z = sb("Z", [128, 16, L], F32, last)
        G2 = G16[:, :].rearrange("p (m t) -> p m t", m=16)
        tZ = [None] * 16
        base2 = []

        def z_out(m, b, p, n, free):
            if m < 8 and n == L:
                while 7 not in swapped:
                    yield
                free = swapped[7]
            while hr in active and m >= 8:
                yield
            if not base2 and m >= 8:
                base2.extend([(V.sem, V.count), (S.sem, S.count), (G.sem, G.count), (PE.sem, PE.count)])
            tZ[m] = S.put(lambda e: e.activation(Z[:, m, 0:n], b.ap[:, 0:n], ACT.Copy), p, free)
            b.free = [tZ[m]]
            yield
            _, t = square_up(m == 0, Z[:, m, 0:n], tZ[m], n)
            if m == 15:
                sums["z", n] = t
            yield

        yfull = lambda k: [(YH[:, k, :], YL[:, k, :], slice(0, L))]
        gemm_lead("w_aout", range(4), (0, 1), yfull, lambda k: got(tY, k), lambda m, b, p: z_out(m, b, p, L, base2))
        for m in range(4, 16):
            b, p = gemm("w_aout", m, (0, 1), yfull, lambda k: tY[k], L)
            spawn(z_out(m, b, p, L, base2))
        pe_ao = p
        tA[:] = [None] * 16
        tY[:] = [None] * 16
        finish(*active)

        r, t_r = inv_root(2048, L, sums["z", L])

        def low(k, th):
            tl = V.put(lambda e: e.scalar_tensor_tensor(
                out=AL[:, k, :], in0=H[:, k, :], scalar=col("pre_g", 16 + k), in1=AH[:, k, :].bitcast(F32),
                op0=ALU.mult, op1=ALU.subtract), th, pe_ao)
            tA[k] = [th, tl]

        def onto(r, t_r):
            th = None
            for k in range(16):
                a = V.put(lambda e, k=k: e.tensor_tensor(Z[:, k, :], Z[:, k, :], r.ap[:, 0:L], ALU.mult), t_r)
                tH[k] = V.put(lambda e, k=k: e.scalar_tensor_tensor(out=H[:, k, :], in0=Z[:, k, :],
                                                                    scalar=col("post_g", k), in1=H[:, k, :],
                                                                    op0=ALU.mult, op1=ALU.add), a, tH[k])
                if k:
                    low(k - 1, th)
                th = S.put(lambda e, k=k: e.activation(AH[:, k, :], H[:, k, :], ACT.Identity, scale=col("pre_g", 16 + k)),
                           tH[k], pe_ao)
                _, t = square_up(k == 0, H[:, k, :], tH[k], L)
                if k % 2:
                    yield
            low(15, th)
            r.free = [a]
            z_free.extend([tH[15], a])
            sums["pin"] = t
            yield

        z_free = []
        spawn(onto(r, t_r))
        spawn(row_of("pin", L))

        def pool_out(m, b, p):
            while "pin" not in row_t:
                yield
            u = [tmp.get() for _ in range(2)]
            t = V.put(lambda e: e.tensor_tensor(u[0].ap[:, :], b.ap[:, 0:L], rown.ap[:, :], ALU.mult), p, row_t["pin"],
                      u[0].free)
            b.free = [t]
            rown.free = [t]
            yield
            src, w = u[0].ap, 1
            x = tmp.get()
            for i in range(m // 4 + 1):
                dst = u[1].ap if i % 2 == 0 else x.ap
                lo = 2 * w - 1
                t = V.put(lambda e, dst=dst, src=src, w=w, lo=lo: e.tensor_tensor(
                    dst[:, lo:L], src[:, lo:L], src[:, lo - w:L - w], ALU.add), t, u[1].free if i == 0 else x.free)
                src = dst
                w *= 2
            t = V.put(lambda e, src=src, w=w: e.scalar_tensor_tensor(out=x.ap[:, NM:L], in0=src[:, NM:L],
                                                                     scalar=1.0 / w, in1=u[0].ap[:, NM:L],
                                                                     op0=ALU.mult, op1=ALU.subtract), t, x.free)
            u[0].free = [t]
            u[1].free = [t]
            tY[m] = yield from split_later(x.ap[:, NM:L], YH[:, m, 0:T], YL[:, m, 0:T], t, (pe_ao,))
            x.free = tY[m]
            yield

        row_key[0] = "pin"
        gemm_lead("w_pin", range(4), (0, 1), full, lambda k: got(tA, k), pool_out)
        for m in range(4, 16):
            b, p = gemm("w_pin", m, (0, 1), full, lambda k: tA[k], L)
            spawn(pool_out(m, b, p))
        gbox = {}
        tail = lambda k: [(AH[:, k, NM:L], AL[:, k, NM:L], slice(0, T))]
        for m in range(16):
            b, p = gemm("w_pin", 16 + m, (0, 1), tail, lambda k: [], T)
            spawn(silu2_out(G2[:, m, :], b, p, T, NM, base2, gbox, "g"))
        pe_g = p
        tA[:] = [None] * 16

        def grp_out(m, b, p):
            while len(gbox["g"]) <= m:
                yield
            x = tmp.get()
            a = V.put(lambda e: e.scalar_tensor_tensor(out=x.ap[:, 0:T], in0=b.ap[:, 0:T],
                                                       scalar=vt[:, PB + m:PB + m + 1], in1=G2[:, m, :],
                                                       op0=ALU.mult, op1=ALU.mult), p, x.free, gbox["g"][m:m + 1], t_ps)
            b.free = [a]
            yield
            tA[m] = yield from split_later(x.ap[:, 0:T], AH[:, m, 0:T], AL[:, m, 0:T], a, (pe_g,))
            x.free = tA[m]
            yield

        for g in range(4):
            for mp in range(2):
                s, t_hi, t_lo = use(("w_grp", g, mp))
                for mi in range(2):
                    while all(b.held for b in acc.bufs):
                        step()
                    b = acc.get()
                    for k in range(4):
                        kt = 4 * g + k
                        for q, (w, x, t) in enumerate(((his[s], YH, t_hi), (his[s], YL, None), (los[s], YH, t_lo))):
                            p = PE.put(lambda e, b=b, w=w, x=x, k=k, kt=kt, mi=mi, q=q: e.matmul(
                                b.ap[:, 0:T], w[:, 4 * mi + k, :], x[:, kt, 0:T], start=(k == 0 and q == 0),
                                stop=(k == 3 and q == 2)), t, got(tY, kt), b.free, mark=(k == 3 and q == 2))
                    spawn(grp_out(4 * g + 2 * mp + mi, b, p))
                split_free[s] = [p]
                step()
        gemm_lead("w_pout", range(4), (0, 1), lat, lambda k: got(tA, k), lambda m, b, p: z_out(m, b, p, T, z_free))
        for m in range(4, 16):
            b, p = gemm("w_pout", m, (0, 1), lat, lambda k: tA[k], T)
            spawn(z_out(m, b, p, T, z_free))
        finish(*active)
        r, t_r = inv_root(2048, T, sums["z", T])
        s_out = sem("s_out")
        n_out = 0
        for k in range(16):
            a = V.put(lambda e, k=k, r=r: e.tensor_tensor(Z[:, k, 0:T], Z[:, k, 0:T], r.ap[:, 0:T], ALU.mult), t_r)
            a = V.put(lambda e, k=k: e.scalar_tensor_tensor(out=Z[:, k, 0:T], in0=Z[:, k, 0:T],
                                                            scalar=col("post_g", 16 + k), in1=H[:, k, NM:L],
                                                            op0=ALU.mult, op1=ALU.add), a)
            if k % 4 == 3:
                SP.put(lambda e, k=k: e.dma_start(out_d[:, k - 3:k + 1, :], Z[:, k - 3:k + 1, 0:T]), a, mark=False,
                       inc=(s_out, 16))
                n_out += 16
        last.close()
        assert st["use"] == len(plan)

        block = ctx.enter_context(nc.Block())

        @block.sync
        def _(eng):
            SP.run(eng)
            eng.wait_ge(s_out, n_out)

        @block.tensor
        def _(eng):
            PE.run(eng)

        @block.vector
        def _(eng):
            V.run(eng)

        @block.scalar
        def _(eng):
            S.run(eng)

        @block.gpsimd
        def _(eng):
            G.run(eng)


def _columns(v):
    return np.ascontiguousarray(v).reshape(-1, 128).T


def _units(w):
    k, m = w.shape
    return w.reshape(k // 1024, KU, 128, m // 128, 128).transpose(3, 0, 2, 1, 4).reshape(m // 128, k // 1024, 128, 1024)


def _tokens(x):
    return x.T.reshape(-1, 128, x.shape[0]).transpose(1, 0, 2)


def _constants():
    c = np.zeros((128, NCONST), np.float32)
    c[:, C_ID:C_ID + 128] = np.eye(128, dtype=np.float32)
    q = np.arange(64)
    start = np.clip(q - 8, 0, 48)[:, None]
    off = q[None, :] - start
    mask = np.where((off >= 0) & (off < 16), 0.0, NEG).astype(np.float32)
    c[:, C_MASK:C_MASK + 64] = np.concatenate([mask[::-1], mask[::-1]], 0)
    inv = np.float32(500000.0) ** (-np.arange(0, 32, 2, dtype=np.float32) / np.float32(32))
    ang = np.arange(L, dtype=np.float32)[:, None] * inv[None, :]
    cos, sin = np.cos(ang).T, np.sin(ang).T
    c[0:32, C_COS:C_COS + L] = np.concatenate([cos, cos], 0)
    c[0:32, C_SIN:C_SIN + L] = np.concatenate([-sin, sin], 0)
    c[:, C_ONE] = 1.0
    c[:, C_EPS] = EPS
    return c


def laid_out(inputs):
    a = {k: np.asarray(v) for k, v in inputs.items()}
    parts = {
        "c": a["c"], "cc": a["c_ctx"], "b_mod": a["b_mod"], "n1g": a["norm1_g"], "n2g": a["norm2_g"],
        "b_in": a["b_in"], "conv_b": a["conv_b"], "cln_g": a["conv_ln_g"], "cln_b": a["conv_ln_b"],
        "conv_w": a["conv_w"], "sln_g": a["sgu_ln_g"], "sln_b": a["sgu_ln_b"], "b_o": a["b_o"],
        "b_ff1": a["b_ff1"], "b_ff2": a["b_ff2"], "fin_g": a["final_g"], "pre_g": a["pre_norm_g_2"],
        "post_g": a["post_norm_g_2"], "sub_g": a["attn_subln_g_2"], "p_scale": a["pool_scale_2"],
        "lam": np.concatenate([a["attn_lambda_q1_2"], a["attn_lambda_q2_2"], a["attn_lambda_k1_2"],
                               a["attn_lambda_k2_2"]], 0),
    }
    vec = np.concatenate([_columns(parts[n]) for n, _ in VECS], 1)
    rpb = np.zeros((16, 15, 128), np.float32)
    rpb[:, :, 48:79] = a["na_rpb"][0]
    arrays = {
        "vec": vec,
        "cst": _constants(),
        "x": _tokens(a["x"][0]),
        "ctx": _tokens(a["ctx"][0]),
        "meta": _tokens(a["meta_tokens_2"]),
        "rpb": rpb,
        "sgu_w": a["sgu_w"][0].transpose(2, 0, 1),
        "sgu_b": a["sgu_b"][0],
        "w_mod": a["w_mod"][0].reshape(8, 2, 128, 24, 512).transpose(3, 0, 2, 1, 4).reshape(24, 8, 128, 1024),
        "w_grp": a["pool_w_group_2"][0].reshape(4, 4, 128, 2, 2, 128).transpose(0, 3, 2, 4, 1, 5)
        .reshape(4, 2, 128, 1024),
    }
    for name, src in (("w_in", "w_in"), ("w_sgu", "w_sgu_out"), ("w_na", "w_na_out"), ("w_conv", "w_conv_out"),
                      ("w_o", "w_o"), ("w_ff1", "w_ff1"), ("w_ff2", "w_ff2"), ("w_ain", "attn_w_in_2"),
                      ("w_aout", "attn_w_out_2"), ("w_pin", "pool_w_in_2"), ("w_pout", "pool_w_out_2")):
        arrays[name] = _units(a[src][0])
    return {name: np.ascontiguousarray(v) for name, v in arrays.items()}


def kernel(**inputs):
    import concourse.bacc as _bacc
    from concourse.bass_utils import run_bass_kernel_spmd as _run

    arrays = laid_out(inputs)
    nc = _bacc.Bacc("TRN2", target_bir_lowering=False, num_devices=1)
    aps, feed = {}, {}
    for name, v in arrays.items():
        feed[f"in_{name}"] = v
        aps[name] = nc.dram_tensor(f"in_{name}", v.shape, F32, kind="ExternalInput").ap()
    out = nc.dram_tensor("out_0", (128, 16, T), F32, kind="ExternalOutput").ap()
    build(nc, aps, out)
    r = _run(nc, [feed], core_ids=[0])
    got = np.asarray(r.results[0]["out_0"])
    return np.ascontiguousarray(got.transpose(2, 1, 0).reshape(1, T, D))
```
